# Optimizing a Trainium2 kernel written in Bass

```python
import jax, jax.numpy as jnp
from jax import lax
import numpy as np

D_MODEL = 2048
BATCH = 1
SEQ = 256
DEPTH = 2

GRID_W = 64
Q_BLOCK = 128
NORM_EPS = 1e-6
ROPE_THETA = 10000.0

HEAD_DIM = 128
ATTN_HEADS = D_MODEL // (2 * HEAD_DIM)
ATTN_KV_HEADS = ATTN_HEADS // 4
ATTN_WIDTH = ATTN_HEADS * HEAD_DIM
KV_WIDTH = ATTN_KV_HEADS * HEAD_DIM
CONV_GROUPS = 8
CONV_WIDTH = D_MODEL // 2
CONV_K = 3
IN0_WIDTH = ATTN_WIDTH + 2 * KV_WIDTH + 3 * CONV_WIDTH
MIX0_WIDTH = ATTN_WIDTH + CONV_WIDTH
MLA_HEADS = D_MODEL // 128
MLA_NOPE = 128
MLA_ROPE = 64
MLA_V = 128
Q_LORA = 512
KV_LORA = 512
MLA_DOWN_WIDTH = Q_LORA + KV_LORA + MLA_ROPE
D_FF = 4 * D_MODEL

N_EVEN = (DEPTH + 1) // 2
N_ODD = DEPTH // 2

kernel_name = 'hybrid_gqa_shortconv_mla_encoder'

def rms_norm(x, g):
    xf = x.astype(jnp.float32)
    y = xf * lax.rsqrt(jnp.mean(xf * xf, axis=-1, keepdims=True) + NORM_EPS)
    return (y * g.astype(jnp.float32)).astype(x.dtype)

def axial_rope_angles(seq, rot_dim):
    rows = seq // GRID_W
    row = jnp.repeat(jnp.arange(rows, dtype=jnp.float32), GRID_W)
    col = jnp.tile(jnp.arange(GRID_W, dtype=jnp.float32), rows)
    axis_dim = rot_dim // 2
    inv_freq = ROPE_THETA ** (-jnp.arange(0, axis_dim, 2, dtype=jnp.float32) / axis_dim)
    ang = jnp.concatenate([row[:, None] * inv_freq, col[:, None] * inv_freq], axis=-1)
    return jnp.cos(ang), jnp.sin(ang)

def apply_rope(x, cos, sin):
    xf = x.astype(jnp.float32).reshape(x.shape[:-1] + (-1, 2))
    x1, x2 = xf[..., 0], xf[..., 1]
    out = jnp.stack([x1 * cos - x2 * sin, x1 * sin + x2 * cos], axis=-1)
    return out.reshape(x.shape).astype(x.dtype)

def gqa_attention(q, k, v):
    b, s, h, dh = q.shape
    kvh = k.shape[2]
    g = h // kvh
    nblk = s // Q_BLOCK
    qb = q.reshape(b, nblk, Q_BLOCK, kvh, g, dh).transpose(1, 0, 2, 3, 4, 5)
    scale = dh ** -0.5

    def block(q_blk):
        sc = jnp.einsum('bqkgd,bskd->bkgqs', q_blk, k).astype(jnp.float32) * scale
        p = jax.nn.softmax(sc, axis=-1).astype(v.dtype)
        return jnp.einsum('bkgqs,bskd->bqkgd', p, v)

    out = lax.map(block, qb)
    return out.transpose(1, 0, 2, 3, 4, 5).reshape(b, s, h * dh)

def mla_attention(q_nope, q_rope, k_nope, k_rope, v):
    b, s, h, dn = q_nope.shape
    dr = q_rope.shape[-1]
    nblk = s // Q_BLOCK
    qn = q_nope.reshape(b, nblk, Q_BLOCK, h, dn).transpose(1, 0, 2, 3, 4)
    qr = q_rope.reshape(b, nblk, Q_BLOCK, h, dr).transpose(1, 0, 2, 3, 4)
    scale = (dn + dr) ** -0.5

    def block(args):
        qn_blk, qr_blk = args
        sc = (jnp.einsum('bqhd,bshd->bhqs', qn_blk, k_nope)
              + jnp.einsum('bqhr,bsr->bhqs', qr_blk, k_rope)).astype(jnp.float32) * scale
        p = jax.nn.softmax(sc, axis=-1).astype(v.dtype)
        return jnp.einsum('bhqs,bshd->bqhd', p, v)

    out = lax.map(block, (qn, qr))
    return out.transpose(1, 0, 2, 3, 4).reshape(b, s, h * v.shape[-1])

def even_mixer(h, w_in, q_norm_g, k_norm_g, conv_w, w_out, cos, sin):
    b, s, _ = h.shape
    proj = h @ w_in
    o1 = ATTN_WIDTH
    o2 = o1 + KV_WIDTH
    o3 = o2 + KV_WIDTH
    o4 = o3 + CONV_WIDTH
    o5 = o4 + CONV_WIDTH
    q, k, v, gate_b, gate_c, u = jnp.split(proj, [o1, o2, o3, o4, o5], axis=-1)
    cos_h, sin_h = cos[:, None, :], sin[:, None, :]
    q = apply_rope(rms_norm(q.reshape(b, s, ATTN_HEADS, HEAD_DIM), q_norm_g), cos_h, sin_h)
    k = apply_rope(rms_norm(k.reshape(b, s, ATTN_KV_HEADS, HEAD_DIM), k_norm_g), cos_h, sin_h)
    v = v.reshape(b, s, ATTN_KV_HEADS, HEAD_DIM)
    attn = gqa_attention(q, k, v)
    conv_in = gate_c * u
    conv = lax.conv_general_dilated(
        conv_in, conv_w[:, None, :].astype(conv_in.dtype), window_strides=(1,), padding='SAME',
        dimension_numbers=('NWC', 'WIO', 'NWC'), feature_group_count=CONV_WIDTH)
    sconv = gate_b * conv
    return jnp.concatenate([attn, sconv], axis=-1) @ w_out

def odd_mixer(h, w_down, q_lat_g, kv_lat_g, w_uq, w_ukv, w_o, cos, sin):
    b, s, _ = h.shape
    lat = h @ w_down
    c_q, c_kv, k_rope = jnp.split(lat, [Q_LORA, Q_LORA + KV_LORA], axis=-1)
    q = (rms_norm(c_q, q_lat_g) @ w_uq).reshape(b, s, MLA_HEADS, MLA_NOPE + MLA_ROPE)
    q_nope, q_rope = q[..., :MLA_NOPE], q[..., MLA_NOPE:]
    q_rope = apply_rope(q_rope, cos[:, None, :], sin[:, None, :])
    k_rope = apply_rope(k_rope, cos, sin)
    kv = (rms_norm(c_kv, kv_lat_g) @ w_ukv).reshape(b, s, MLA_HEADS, MLA_NOPE + MLA_V)
    k_nope, v = kv[..., :MLA_NOPE], kv[..., MLA_NOPE:]
    attn = mla_attention(q_nope, q_rope, k_nope, k_rope, v)
    return attn @ w_o

def squared_relu_mlp(h, w_up, w_dn):
    return jnp.square(jax.nn.relu(h @ w_up)) @ w_dn

def setup_inputs(seed: int = 0) -> dict:
    key = jax.random.key(seed)
    ks = jax.random.split(key, 20)

    def w(k, shape, fan_in):
        return jax.random.normal(k, shape, jnp.float32) * (fan_in ** -0.5)

    def gain(k, shape):
        return 1.0 + 0.02 * jax.random.normal(k, shape, jnp.float32)

    return {
        'x': jax.random.normal(ks[0], (BATCH, SEQ, D_MODEL), jnp.float32),
        'even_norm_g': gain(ks[1], (N_EVEN, D_MODEL)),
        'even_w_in': w(ks[2], (N_EVEN, D_MODEL, IN0_WIDTH), D_MODEL),
        'even_q_norm_g': gain(ks[3], (N_EVEN, HEAD_DIM)),
        'even_k_norm_g': gain(ks[4], (N_EVEN, HEAD_DIM)),
        'even_conv_w': w(ks[5], (N_EVEN, CONV_K, CONV_WIDTH), CONV_K),
        'even_w_out': w(ks[6], (N_EVEN, MIX0_WIDTH, D_MODEL), MIX0_WIDTH),
        'odd_norm_g': gain(ks[7], (N_ODD, D_MODEL)),
        'odd_w_down': w(ks[8], (N_ODD, D_MODEL, MLA_DOWN_WIDTH), D_MODEL),
        'odd_q_lat_g': gain(ks[9], (N_ODD, Q_LORA)),
        'odd_kv_lat_g': gain(ks[10], (N_ODD, KV_LORA)),
        'odd_w_uq': w(ks[11], (N_ODD, Q_LORA, MLA_HEADS * (MLA_NOPE + MLA_ROPE)), Q_LORA),
        'odd_w_ukv': w(ks[12], (N_ODD, KV_LORA, MLA_HEADS * (MLA_NOPE + MLA_V)), KV_LORA),
        'odd_w_o': w(ks[13], (N_ODD, MLA_HEADS * MLA_V, D_MODEL), MLA_HEADS * MLA_V),
        'mlp_norm_g': gain(ks[14], (DEPTH, D_MODEL)),
        'mlp_w_up': w(ks[15], (DEPTH, D_MODEL, D_FF), D_MODEL),
        'mlp_w_down': w(ks[16], (DEPTH, D_FF, D_MODEL), D_FF),
        'final_norm_g': gain(ks[17], (D_MODEL,)),
    }

def reference(x, even_norm_g, even_w_in, even_q_norm_g, even_k_norm_g, even_conv_w, even_w_out,
              odd_norm_g, odd_w_down, odd_q_lat_g, odd_kv_lat_g, odd_w_uq, odd_w_ukv, odd_w_o,
              mlp_norm_g, mlp_w_up, mlp_w_down, final_norm_g):
    s = x.shape[1]
    cos_a, sin_a = axial_rope_angles(s, HEAD_DIM)
    cos_c, sin_c = axial_rope_angles(s, MLA_ROPE)
    h = x
    for layer in range(DEPTH):
        i = layer // 2
        if layer % 2 == 0:
            h = h + even_mixer(rms_norm(h, even_norm_g[i]), even_w_in[i], even_q_norm_g[i],
                               even_k_norm_g[i], even_conv_w[i], even_w_out[i], cos_a, sin_a)
        else:
            h = h + odd_mixer(rms_norm(h, odd_norm_g[i]), odd_w_down[i], odd_q_lat_g[i],
                              odd_kv_lat_g[i], odd_w_uq[i], odd_w_ukv[i], odd_w_o[i], cos_c, sin_c)
        h = h + squared_relu_mlp(rms_norm(h, mlp_norm_g[layer]), mlp_w_up[layer], mlp_w_down[layer])
    return rms_norm(h, final_norm_g)


_drawn_inputs = setup_inputs


def setup_inputs(seed=0):
    import zlib

    import numpy as np

    out = dict(_drawn_inputs(seed))
    spreads = {}
    factors = {'even_q_norm_g': 8.0,
     'even_k_norm_g': 8.0,
     'odd_norm_g': 8.0,
     'odd_q_lat_g': 8.0,
     'odd_kv_lat_g': 8.0,
     'final_norm_g': 2.831}
    for name, (base, spread) in spreads.items():
        noise = np.random.default_rng([zlib.crc32(name.encode()), seed]).standard_normal(out[name].shape)
        drawn = base * np.exp(spread * noise) if base else spread * noise
        out[name] = __import__('jax').numpy.asarray(drawn.astype(out[name].dtype))
    for name, factor in factors.items():
        out[name] = (out[name] * factor).astype(out[name].dtype)
    return out
```

```python
from contextlib import ExitStack

import concourse.bass as bass
from concourse import mybir
from concourse.alu_op_type import AluOpType as ALU

ACT = mybir.ActivationFunctionType
F32 = mybir.dt.float32
F32R = mybir.dt.float32r
AX_X = mybir.AxisListType.X

P = 128
D = 2048
TOK = 2
T = TOK * P
KT = D // P
NORM_EPS = 1e-6

HEADS_A, KV_A, HD = 8, 2, 128
QK_A = (HEADS_A + KV_A) * HD
IN_A = 4608
B_AT, C_AT, U_AT = 1536, 2560, 3584
HEADS_C, NOPE, ROPE = 16, 128, 64
QH = NOPE + ROPE
LORA = 512
D_FF = 8192

UNIT = 2048
RAW = 4
SPLIT = 2

U_IN = 0
U_OUT = U_IN + 4 * (IN_A // 512)
U_UP = [0, 0]
U_DN = [0, 0]
U_UP[0] = U_OUT + KT
U_DN[0] = U_UP[0] + 4 * (D_FF // 512)
U_KR = U_DN[0] + D_FF // P
U_CKV = U_KR + 1
U_CQ = U_CKV + 4
U_QKV = U_CQ + 4
U_O = U_QKV + HEADS_C
U_UP[1] = U_O + KT
U_DN[1] = U_UP[1] + 4 * (D_FF // 512)
U_END = U_DN[1] + D_FF // P

K_OUT, K_DN0, K_O, K_DN1 = 0, KT, KT + D_FF // P, 2 * KT + D_FF // P

X_BEFORE = {"mix0": 0, "mlp0": 16, "mix1": 32, "lat": 48, "mlp1": 56}
STAGES = ["mix0", "mlp0", "mix1", "mlp1", "final"]

G_ROW = {"mix0": 0, "mlp0": 16, "mix1": 32, "mlp1": 48, "q_lat": 64, "kv_lat": 68, "taps": 72}
G_ROWS = 96


HEADS_BASE = 1


def at(c, it=None, per=0):
    return c if it is None else it * per + c


def landed_count(u, it=None, per=0):
    return at(16 * (u // RAW + 1), it, 16 * per // RAW)


def build(nc, A, out):
    ctx = ExitStack()
    with ctx:
        def sb(name, shape, dt=F32):
            return ctx.enter_context(nc.sbuf_tensor(name, shape, dt))

        def sem(name):
            return ctx.enter_context(nc.semaphore(name))

        ps = ctx.enter_context(nc.psum_tensor("ps", [P, 8 * 512], F32))
        h = sb("h", [P, TOK, D])
        xs = sb("xs", [P, KT, 2, T], F32R)
        raw = sb("raw", [P, RAW, UNIT])
        w_hi = sb("w_hi", [P, SPLIT, UNIT], F32R)
        w_lo = sb("w_lo", [P, SPLIT, UNIT], F32R)
        js = sb("js", [P, SPLIT, 2, T], F32R)
        big = sb("big", [P, 18432])
        work = sb("work", [P, 3072])
        stage = sb("stage", [P, 2048])
        ident = sb("ident", [P, P])
        gain_rows = sb("gain_rows", [G_ROWS, P])
        gains = sb("gains", [P, G_ROWS])
        rope_c = sb("rope_c", [P, 2, TOK, ROPE // 2])
        krT = sb("krT", [ROPE, T])
        sumsq = sb("sumsq", [P, 5, TOK])
        meansq = sb("meansq", [P, 5, TOK])
        rms = sb("rms", [P, 5, TOK])
        rms2 = sb("rms2", [P, 2, TOK])
        half = sb("half", [P, 24])
        lat_ss = sb("lat_ss", [P, 2, TOK])
        lat_t = sb("lat_t", [P, 3, 2, TOK])
        lat_s = sb("lat_s", [P, 2, TOK])
        head_ms = sb("head_ms", [P, 2 * 10])
        head_r = sb("head_r", [P, 2, 10])
        nmax = sb("nmax", [P, 2, 2])
        rsum = sb("rsum", [P, 2, 2])
        rrec = sb("rrec", [P, 2, 2])

        feat = big[:, 0:64 * T]
        projA = big[:, 4096:4096 + 2 * IN_A].rearrange("p (t c) -> p t c", t=TOK)
        tmpA = big[:, 13312:13312 + 2 * QK_A]
        kT = big[:, 15872:15872 + KV_A * T]
        ropeA = big[:, 16384:16640].rearrange("p (s t c) -> p s t c", s=2, t=TOK)
        gqk = big[:, 16640:16896]
        lat = big[:, 0:2048].rearrange("p (w t c) -> p w t c", w=2, t=TOK)
        kr = big[:, 2048:2176].rearrange("p (t c) -> p t c", t=TOK)
        kr_tmp = big[:, 2176:2432].rearrange("p (j t c) -> p j t c", j=4, t=TOK)
        q_tmp = big[:, 2432:2944].rearrange("p (j c) -> p j c", j=4)
        qC = big[:, 4096:4096 + 2 * 3072].rearrange("p (t c) -> p t c", t=TOK)
        kvC = big[:, 10240:10240 + 2 * 4096].rearrange("p (t c) -> p t c", t=TOK)
        g_final = big[:, 16384:18432]
        final = big[:, 0:2 * D].rearrange("p (t c) -> p t c", t=TOK)

        relu_z, hid = work[:, 0:1024], work[:, 1024:2048]
        qT, knT, qrT = work[:, 0:256], work[:, 256:512], work[0:ROPE, 2560:2816]
        prob = [work[:, 512 + 512 * i:1024 + 512 * i] for i in range(2)]
        probT = work[:, 1536:2048]
        BT = [work[:, 2048 + 256 * i:2304 + 256 * i] for i in range(2)]
        cuT = sb("cuT", [P, 2, T + 2])

        raw_landed = [sem(f"raw_landed{i}") for i in range(RAW)]
        const_landed, x_landed, g_landed = sem("const_landed"), sem("x_landed"), sem("g_landed")
        hi_split, lo_split, unit_used = sem("hi_split"), sem("lo_split"), sem("unit_used")
        jit_hi, jit_lo = sem("jit_hi"), sem("jit_lo")
        bank_pass = sem("bank_pass")
        gains_turned, gains_ready = sem("gains_turned"), sem("gains_ready")
        consts_set = sem("consts_set")
        h_ready, h_turned = sem("h_ready"), sem("h_turned")
        xs_hi, xs_lo = sem("xs_hi"), sem("xs_lo")
        squares, ms_ready, rms_ready = sem("squares"), sem("ms_ready"), sem("rms_ready")
        rms2_ready = sem("rms2_ready")
        mix_evac = sem("mix_evac")
        pool_step = sem("pool_step")
        qk_ready = sem("qk_ready")
        k_turned, kT_ready = sem("k_turned"), sem("kT_ready")
        staged, v_staged = sem("staged"), sem("v_staged")
        heads_turned, turned_act, turned_dve = sem("heads_turned"), sem("turned_act"), sem("turned_dve")
        scores_ready, max_ready, exp_ready = sem("scores_ready"), sem("max_ready"), sem("exp_ready")
        recip_ready, probs_ready = sem("recip_ready"), sem("probs_ready")
        probs_turned, probT_ready = sem("probs_turned"), sem("probT_ready")
        heads_out, heads_ready = sem("heads_out"), sem("heads_ready")
        taps, conv_ready = sem("taps"), sem("conv_ready")
        relu_ready, hid_ready = sem("relu_ready"), sem("hid_ready")
        hid_turned, feat_ready = sem("hid_turned"), sem("feat_ready")
        kr_out, kr_roped, kr_turned, krT_ready = sem("kr_out"), sem("kr_roped"), sem("kr_turned"), sem("krT_ready")
        lat_out, lat_sq, lat_turned, lat_scale = sem("lat_out"), sem("lat_sq"), sem("lat_turned"), sem("lat_scale")
        kv_out, q_out, q_prod, q_roped = sem("kv_out"), sem("q_out"), sem("q_prod"), sem("q_roped")
        pool_waited = sem("pool_waited")
        final_ready, stored = sem("final_ready"), sem("stored")

        block = ctx.enter_context(nc.Block())

        K_PHASES = {"out": (U_OUT, K_OUT, KT), "dn0": (U_DN[0], K_DN0, D_FF // P),
                    "o": (U_O, K_O, KT), "dn1": (U_DN[1], K_DN1, D_FF // P)}
        AFTER = {"mlp0": "out", "mix1": "dn0", "mlp1": "o", "final": "dn1"}

        @block.sync
        def _(sp):
            def load(u, src, cols, it=None, per=0):
                if u >= RAW:
                    sp.wait_ge(lo_split, at(u - RAW + 1, it, per))
                s = u % RAW
                dst = raw[:, s, 0:cols]
                if len(src.shape) == 3:
                    dst = dst.rearrange("p (k c) -> p k c", k=src.shape[1])
                sp.dma_start(dst, src).then_inc(raw_landed[s], 16)

            def tiles(w):
                return w.rearrange("(k p) c -> p k c", p=P)

            w = tiles(A["even_w_in"][0])
            for j in range(RAW):
                load(U_IN + j, w[:, 4 * j:4 * j + 4, 0:512], UNIT)
            with nc.sync.Fori(0, IN_A // 512 - 1) as it:
                for j in range(4):
                    load(U_IN + 4 + j, w[:, 4 * j:4 * j + 4, bass.ds(at(512, it, 512), 512)], UNIT, it, 4)

            def k_major(w, u0, n):
                w = w.rearrange("(g k p) c -> p g k c", p=P, k=4)
                with nc.sync.Fori(0, n // 4) as it:
                    for j in range(4):
                        load(u0 + j, w[:, bass.ds(it, 1), j, :].rearrange("p g c -> p (g c)"), UNIT, it, 4)

            def n_major(w, u0, blocks):
                w = tiles(w)
                with nc.sync.Fori(0, blocks) as it:
                    for j in range(4):
                        load(u0 + j, w[:, 4 * j:4 * j + 4, bass.ds(at(0, it, 512), 512)], UNIT, it, 4)

            k_major(A["even_w_out"][0], U_OUT, KT)
            n_major(A["mlp_w_up"][0], U_UP[0], D_FF // 512)
            k_major(A["mlp_w_down"][0], U_DN[0], D_FF // P)
            w = tiles(A["odd_w_down"][0])
            load(U_KR, w[:, :, 2 * LORA:2 * LORA + ROPE], KT * ROPE)
            for j in range(4):
                load(U_CKV + j, w[:, 4 * j:4 * j + 4, LORA:2 * LORA], UNIT)
            for j in range(4):
                load(U_CQ + j, w[:, 4 * j:4 * j + 4, 0:LORA], UNIT)
            wq, wkv = tiles(A["odd_w_uq"][0]), tiles(A["odd_w_ukv"][0])
            with nc.sync.Fori(0, HEADS_C // 4) as it:
                for a in range(2):
                    load(U_QKV + 2 * a, wkv[:, :, bass.ds(at(512 * a, it, 1024), 512)], UNIT, it, 4)
                    load(U_QKV + 2 * a + 1, wq[:, :, bass.ds(at(2 * QH * a, it, 4 * QH), 2 * QH)],
                         8 * QH, it, 4)
            k_major(A["odd_w_o"][0], U_O, KT)
            sp.wait_ge(heads_ready, HEADS_BASE + HEADS_A + HEADS_C)
            sp.dma_start(g_final, A["final_norm_g"].rearrange("(a c) -> a c", a=1)
                         .to_broadcast([P, D])).then_inc(g_landed, 16)
            n_major(A["mlp_w_up"][1], U_UP[1], D_FF // 512)
            k_major(A["mlp_w_down"][1], U_DN[1], D_FF // P)
            for t in range(TOK):
                sp.wait_ge(final_ready, t + 1)
                sp.dma_start(out[0, t * P:(t + 1) * P, :], final[:, t, :]).then_inc(stored, 16)
            sp.wait_ge(stored, 16 * TOK)

        @block.scalar
        def _(act):
            act.dma_start(h[:, 0, :], A["x"][0, 0:P, :]).then_inc(x_landed, 16)
            act.dma_start(h[:, 1, :], A["x"][0, P:T, :]).then_inc(x_landed, 16)
            act.dma_start(ident[:, :], A["ident"]).then_inc(const_landed, 16)
            for name, g in (("mix0", A["even_norm_g"][0]), ("mlp0", A["mlp_norm_g"][0]),
                            ("mix1", A["odd_norm_g"][0]), ("mlp1", A["mlp_norm_g"][1]),
                            ("q_lat", A["odd_q_lat_g"][0]), ("kv_lat", A["odd_kv_lat_g"][0])):
                g = g.rearrange("(k p) -> k p", p=P)
                act.dma_start(gain_rows[G_ROW[name]:G_ROW[name] + g.shape[0], :], g).then_inc(const_landed, 16)
            act.dma_start(gain_rows[G_ROW["taps"]:G_ROWS, :],
                          A["even_conv_w"][0].rearrange("k (c p) -> (k c) p", p=P)).then_inc(const_landed, 16)
            act.dma_start(ropeA, A["rope_a"]).then_inc(const_landed, 16)
            act.dma_start(rope_c[:, :, :, :], A["rope_c"]).then_inc(const_landed, 16)
            act.dma_start(gqk[:, 0:HD], A["even_q_norm_g"].to_broadcast([P, HD])).then_inc(const_landed, 16)
            act.dma_start(gqk[:, HD:2 * HD], A["even_k_norm_g"].to_broadcast([P, HD])).then_inc(const_landed, 16)

            def hi(u, it=None, per=0, cols=UNIT):
                act.wait_ge(raw_landed[u % RAW], landed_count(u, it, per))
                if u >= SPLIT:
                    act.wait_ge(unit_used, at(u - SPLIT + 1, it, per))
                nc.scalar.activation(w_hi[:, u % SPLIT, 0:cols], raw[:, u % RAW, 0:cols],
                                     ACT.Copy).then_inc(hi_split, 1)

            def turn_in(name):
                s, x0 = STAGES.index(name), X_BEFORE[name]
                for n in range(4):
                    act.wait_ge(h_turned, 4 * s + n + 1)
                    for k in range(4 * n, 4 * n + 4):
                        nc.scalar.activation(xs[:, k, 0, :], ps[:, k * T:(k + 1) * T], ACT.Copy,
                                             scale=gains[:, G_ROW[name] + k:G_ROW[name] + k + 1]
                                             ).then_inc(xs_hi, 1)
                    if n == 1:
                        hi({"mix0": U_IN, "mlp0": U_UP[0], "mix1": U_KR, "mlp1": U_UP[1]}[name] + 1)
                sum_squares(s)

            def sum_squares(s):
                for t in range(TOK):
                    if s or t:
                        act.wait_ge(squares, TOK * s + t)
                    nc.scalar.activation(work[:, 0:D], h[:, t, :], ACT.Square,
                                         accum_out=sumsq[:, s, t:t + 1]).then_inc(squares, 1)

            def k_major(name, src_ready, skip_next=False):
                u0, k0, n = K_PHASES[name]

                def jit(k, it=None):
                    if k0 + k >= SPLIT:
                        act.wait_ge(unit_used, at(u0 + k - SPLIT + 1, it, 4))
                    nc.scalar.activation(js[:, k % SPLIT, 0, :], feat[:, bass.ds(at(k * T, it, 4 * T), T)],
                                         ACT.Copy).then_inc(jit_hi, 1)

                src_ready(act)
                jit(0)
                jit(1)
                with nc.scalar.Fori(0, n // 4 - 1) as it:
                    for j in range(4):
                        jit(j + 2, it)
                        hi(u0 + j + 2, it, 4)
                for j in range(n - 4, n):
                    if j + 2 < n:
                        jit(j + 2)
                        hi(u0 + j + 2)
                    elif j + 2 == n and not skip_next:
                        hi(u0 + n, cols=KT * ROPE if u0 + n == U_KR else UNIT)

            def attention(n, h0, latent):
                def copies(m, it=None):
                    act.wait_ge(heads_turned, at(h0 + m + 1, it, 2))
                    if latent:
                        nc.scalar.activation(work[:, 0:512], ps[:, 0:512], ACT.Copy).then_inc(turned_act, 1)
                    else:
                        nc.scalar.activation(qT, ps[:, 0:256], ACT.Copy)
                        if m >= 2:
                            act.wait_ge(conv_ready, at(m - 1, it, 2))
                        nc.scalar.activation(BT[m % 2], ps[:, 2560:2816], ACT.Copy).then_inc(turned_act, 1)

                def exps(m, it=None):
                    act.wait_ge(max_ready, at(h0 + m + 1, it, 2))
                    if h0 + m >= 2:
                        act.wait_ge(probs_turned, at(h0 + m - 1, it, 2))
                    b = 1024 + 512 * (m % 2)
                    for q in range(2):
                        ins = nc.scalar.activation(prob[m % 2][:, q * T:(q + 1) * T],
                                                   ps[:, b + q * T:b + (q + 1) * T], ACT.Exp,
                                                   bias=nmax[:, m % 2, q:q + 1],
                                                   accum_out=rsum[:, m % 2, q:q + 1])
                    ins.then_inc(exp_ready, 1)

                def turned(m, it=None):
                    act.wait_ge(probs_turned, at(h0 + m + 1, it, 2))
                    nc.scalar.activation(probT, ps[:, 2048:2560], ACT.Copy).then_inc(probT_ready, 1)

                for m, it in turns(nc.scalar, n):
                    if 0 <= m + 1 < n:
                        copies(m + 1, it)
                    if 0 <= m < n:
                        exps(m, it)
                    if 0 <= m - 1 < n:
                        turned(m - 1, it)

            def mlp_up(layer):
                u0, f0 = U_UP[layer], 16 * layer

                def move(n, it=None):
                    act.wait_ge(hid_turned, at(f0 + n + 1, it, 2))
                    nc.scalar.activation(feat[:, bass.ds(at(n * 4 * T, it, 8 * T), 4 * T)],
                                         ps[:, 2048:3072], ACT.Copy).then_inc(feat_ready, 1)

                def block_pair(n, it=None, first=False):
                    for a in range(2):
                        u = u0 + 4 * (n + a)
                        for j in range(3):
                            hi(u + j + 2, it, 8)
                        if not (first and a == 0):
                            move(n + a - 1, it)
                        hi(u + 5, it, 8)
                        act.wait_ge(unit_used, at(u + 4, it, 8))
                        nc.scalar.activation(relu_z, ps[:, 1024 * a:1024 * a + 1024],
                                             ACT.Relu).then_inc(relu_ready, 1)

                block_pair(0, first=True)
                with nc.scalar.Fori(0, D_FF // 1024 - 1) as it:
                    block_pair(2, it)
                move(D_FF // 512 - 1)

            hi(U_IN)
            act.wait_ge(gains_turned, 1)
            nc.scalar.activation(gains[:, :], ps[:, 3584:3584 + G_ROWS], ACT.Copy).then_inc(gains_ready, 1)
            act.wait_ge(gains_ready, 1)
            turn_in("mix0")
            act.wait_ge(rms_ready, 1)
            with nc.scalar.Fori(0, 3) as it:
                for b in range(3):
                    for j in range(4):
                        hi(U_IN + 4 * b + j + 2, it, 12)
                    act.wait_ge(unit_used, at(U_IN + 4 * b + 4, it, 12))
                    for t in range(TOK):
                        ins = nc.scalar.activation(projA[:, t, bass.ds(at(512 * b, it, 1536), 512)],
                                                   ps[:, 1024 * b + 512 * t:1024 * b + 512 * t + 512],
                                                   ACT.Copy, scale=rms[:, 0, t:t + 1])
                    ins.then_inc(mix_evac, 1)
            act.wait_ge(k_turned, 1)
            nc.scalar.activation(kT, ps[:, 3072:3584], ACT.Copy).then_inc(kT_ready, 1)
            attention(HEADS_A, 0, False)

            def mixed(eng, heads, conv):
                eng.wait_ge(heads_ready, HEADS_BASE + heads)
                eng.wait_ge(conv_ready, conv)

            k_major("out", lambda e: mixed(e, HEADS_A, 8))
            turn_in("mlp0")
            mlp_up(0)
            k_major("dn0", lambda e: e.wait_ge(feat_ready, 16))
            turn_in("mix1")

            def latent_out(which, bank):
                nc.scalar.activation(lat[:, which, :, :].rearrange("p t c -> p (t c)"),
                                     ps[:, 512 * bank:512 * bank + 1024], ACT.Copy).then_inc(lat_out, 1)
                for t in range(TOK):
                    if which == 0 or t:
                        act.wait_ge(lat_sq, (2 if which == 0 else 0) + t)
                    nc.scalar.activation(work[:, 0:512], ps[:, 512 * (bank + t):512 * (bank + t) + 512],
                                         ACT.Square, accum_out=lat_ss[:, which, t:t + 1]).then_inc(lat_sq, 1)

            hi(U_KR + 2)
            act.wait_ge(unit_used, U_KR + 1)
            act.wait_ge(rms_ready, 3)
            for t in range(TOK):
                ins = nc.scalar.activation(kr[:, t, :], ps[:, 512 * (6 + t):512 * (6 + t) + ROPE], ACT.Copy,
                                           scale=rms[:, 2, t:t + 1])
            ins.then_inc(kr_out, 1)
            for j in range(4):
                hi(U_CKV + 2 + j)
            act.wait_ge(unit_used, U_CKV + 4)
            latent_out(1, 0)
            hi(U_CQ + 2)
            hi(U_CQ + 3)
            hi(U_CQ + 4)
            act.wait_ge(unit_used, U_CQ + 4)
            latent_out(0, 2)
            for which, name, k0 in ((1, "kv_lat", 0), (0, "q_lat", 4)):
                act.wait_ge(lat_turned, 2 - which)
                for k in range(4):
                    b = 2048 + 1024 * (1 - which) + k * T
                    nc.scalar.activation(xs[:, k0 + k, 0, :], ps[:, b:b + T], ACT.Copy,
                                         scale=gains[:, G_ROW[name] + k:G_ROW[name] + k + 1]
                                         ).then_inc(xs_hi, 1)
            act.wait_ge(kr_turned, 1)
            nc.scalar.activation(krT[:, :], ps[0:ROPE, 0:T], ACT.Copy).then_inc(krT_ready, 1)
            hi(U_CQ + 5, cols=8 * QH)
            act.wait_ge(lat_scale, 1)
            with nc.scalar.Fori(0, HEADS_C // 4) as it:
                for a in range(2):
                    for q in range(2):
                        u = U_QKV + 2 * a + q
                        hi(u + 2, it, 4, cols=UNIT)
                        act.wait_ge(unit_used, at(u + 1, it, 4))
                        for t in range(TOK):
                            b = 2048 * a + 1024 * q + 512 * t
                            if q:
                                dst = qC[:, t, bass.ds(at(2 * QH * a, it, 4 * QH), 2 * QH)]
                                ins = nc.scalar.activation(dst, ps[:, b:b + 2 * QH], ACT.Copy,
                                                           scale=lat_s[:, 0, t:t + 1])
                            else:
                                dst = kvC[:, t, bass.ds(at(512 * a, it, 1024), 512)]
                                ins = nc.scalar.activation(dst, ps[:, b:b + 512], ACT.Copy,
                                                           scale=lat_s[:, 1, t:t + 1])
                        ins.then_inc(q_out if q else kv_out, 1)
            attention(HEADS_C, HEADS_A, True)
            k_major("o", lambda e: e.wait_ge(heads_ready, HEADS_BASE + HEADS_A + HEADS_C))
            turn_in("mlp1")
            mlp_up(1)
            k_major("dn1", lambda e: e.wait_ge(feat_ready, 32), skip_next=True)
            act.wait_ge(h_ready, 16)
            sum_squares(4)

        @block.vector
        def _(dve):
            def lo(u, it=None, per=0, cols=UNIT):
                dve.wait_ge(hi_split, at(u + 1, it, per))
                nc.vector.tensor_tensor(w_lo[:, u % SPLIT, 0:cols], raw[:, u % RAW, 0:cols],
                                        w_hi[:, u % SPLIT, 0:cols].bitcast(F32),
                                        ALU.subtract).then_inc(lo_split, 1)

            def xs_low(k, x_count, b, g):
                dve.wait_ge(xs_hi, x_count + (k + 1) % 2)
                nc.vector.scalar_tensor_tensor(xs[:, k, 1, :], ps[:, b:b + T], gains[:, g:g + 1],
                                               xs[:, k, 0, :].bitcast(F32), ALU.mult,
                                               ALU.subtract).then_inc(xs_lo, 1)

            def residual(name, n):
                s = STAGES.index(name)
                u0, k0, count = K_PHASES[AFTER[name]]
                if n < 3:
                    dve.wait_ge(bank_pass, 3 * (k0 + count - 1) + n + 1)
                else:
                    dve.wait_ge(unit_used, u0 + count)
                for t in range(TOK):
                    b, to = 1024 * n + 512 * t, h[:, t, 512 * n:512 * n + 512]
                    if name in ("mix1", "final"):
                        ins = nc.vector.scalar_tensor_tensor(to, ps[:, b:b + 512],
                                                             rms2[:, s // 4, t:t + 1], to,
                                                             ALU.mult, ALU.add)
                    else:
                        ins = nc.vector.tensor_tensor(to, ps[:, b:b + 512], to, ALU.add)
                ins.then_inc(h_ready, 1)

            def turn_in(name):
                def low(n):
                    for k in range(4 * n, 4 * n + 4):
                        xs_low(k, X_BEFORE[name] + k + 1, k * T, G_ROW[name] + k)
                if name != "mix0":
                    if name == "mix1":
                        dve.wait_ge(rms2_ready, 1)
                    residual(name, 0)
                    residual(name, 1)
                low(0)
                if name != "mix0":
                    residual(name, 2)
                low(1)
                lo({"mix0": U_IN, "mlp0": U_UP[0], "mix1": U_KR, "mlp1": U_UP[1]}[name] + 1)
                if name != "mix0":
                    residual(name, 3)
                low(2)
                low(3)

            def k_major(name, skip_next=False):
                u0, k0, n = K_PHASES[name]

                def jit(k, it=None):
                    dve.wait_ge(jit_hi, at(k0 + k + 1, it, 4))
                    nc.vector.tensor_tensor(js[:, k % SPLIT, 1, :], feat[:, bass.ds(at(k * T, it, 4 * T), T)],
                                            js[:, k % SPLIT, 0, :].bitcast(F32),
                                            ALU.subtract).then_inc(jit_lo, 1)

                jit(0)
                jit(1)
                with nc.vector.Fori(0, n // 4 - 1) as it:
                    for j in range(4):
                        jit(j + 2, it)
                        lo(u0 + j + 2, it, 4)
                for j in range(n - 4, n):
                    if j + 2 < n:
                        jit(j + 2)
                        lo(u0 + j + 2)
                    elif j + 2 == n and not skip_next:
                        lo(u0 + n, cols=KT * ROPE if u0 + n == U_KR else UNIT)

            def mlp_up(layer):
                u0, f0 = U_UP[layer], 16 * layer

                def block_pair(n, it=None):
                    for a in range(2):
                        u = u0 + 4 * (n + a)
                        for j in range(4):
                            lo(u + j + 2, it, 8)
                        dve.wait_ge(relu_ready, at(f0 + n + a + 1, it, 2))
                        nc.vector.tensor_tensor(hid, ps[:, 1024 * a:1024 * a + 1024], relu_z,
                                                ALU.mult).then_inc(hid_ready, 1)

                with nc.vector.Fori(0, D_FF // 1024) as it:
                    block_pair(0, it)

            def attention(n, h0, latent):
                def copies(m, it=None):
                    dve.wait_ge(heads_turned, at(h0 + m + 1, it, 2))
                    if latent:
                        nc.vector.tensor_copy(qrT, ps[0:ROPE, 512:768]).then_inc(turned_dve, 1)
                    else:
                        nc.vector.tensor_copy(cuT[:, m % 2, 1:T + 1], ps[:, 512:768]).then_inc(turned_dve, 1)

                def conv(m, it=None):
                    y = feat[:, bass.ds(at((8 + m) * T, it, 2 * T), T)]
                    dve.wait_ge(turned_dve, at(m + 1, it, 2))

                    def tap(k):
                        g = G_ROW["taps"] + 8 * k + m
                        return gains[:, bass.ds(at(g, it, 2), 1)] if it is not None else gains[:, g:g + 1]
                    src = cuT[:, m % 2, :]
                    nc.vector.tensor_scalar(y, src[:, 1:T + 1], tap(1), None, ALU.mult).then_inc(taps, 1)
                    for i, k in ((1, 0), (2, 2)):
                        dve.wait_ge(taps, at(3 * m + i, it, 6))
                        nc.vector.scalar_tensor_tensor(y, src[:, k:T + k], tap(k), y, ALU.mult,
                                                       ALU.add).then_inc(taps, 1)

                def maxima(m, it=None):
                    dve.wait_ge(scores_ready, at(h0 + m + 1, it, 2))
                    b = 1024 + 512 * (m % 2)
                    nc.vector.tensor_reduce(nmax[:, m % 2, :],
                                            ps[:, b:b + 512].rearrange("p (q c) -> p q c", q=2),
                                            AX_X, ALU.max, negate=True).then_inc(max_ready, 1)

                def normalise(m, it=None):
                    dve.wait_ge(exp_ready, at(h0 + m + 1, it, 2))
                    nc.vector.reciprocal(rrec[:, m % 2, :], rsum[:, m % 2, :]).then_inc(recip_ready, 1)
                    dve.wait_ge(recip_ready, at(h0 + m + 1, it, 2))
                    for q in range(2):
                        pr = prob[m % 2][:, q * T:(q + 1) * T]
                        ins = nc.vector.tensor_scalar(pr, pr, rrec[:, m % 2, q:q + 1], None, ALU.mult)
                    ins.then_inc(probs_ready, 1)

                def take(m, it=None):
                    dve.wait_ge(heads_out, at(h0 + m + 1, it, 2))
                    nc.vector.tensor_copy(feat[:, bass.ds(at(m * T, it, 2 * T), T)],
                                          ps[:, 3072:3328]).then_inc(heads_ready, 1)

                for m, it in turns(nc.vector, n):
                    if 0 <= m < n:
                        maxima(m, it)
                    if 0 <= m + 1 < n:
                        copies(m + 1, it)
                    if 0 <= m < n and not latent:
                        conv(m, it)
                    if 0 <= m < n:
                        normalise(m, it)
                    if 0 <= m - 2 < n:
                        take(m - 2, it)

            nc.vector.memset(cuT[:, :, :], 0.0).then_inc(consts_set, 1)
            lo(U_IN)
            dve.wait_ge(gains_ready, 1)
            turn_in("mix0")
            with nc.vector.Fori(0, IN_A // 512) as it:
                for j in range(4):
                    lo(U_IN + j + 2, it, 4)
            dve.wait_ge(consts_set, 1)
            dve.wait_ge(kT_ready, 1)
            dve.sem_inc(heads_ready, HEADS_BASE)
            attention(HEADS_A, 0, False)
            dve.wait_ge(conv_ready, 8)
            dve.wait_ge(heads_ready, HEADS_BASE + HEADS_A)
            k_major("out")
            turn_in("mlp0")
            mlp_up(0)
            k_major("dn0")
            turn_in("mix1")
            lo(U_KR + 2)
            for j in range(4):
                lo(U_CKV + 2 + j)
            for j in range(3):
                lo(U_CQ + 2 + j)
            for i, (name, k0) in enumerate((("kv_lat", 0), ("q_lat", 4))):
                for k in range(4):
                    xs_low(k0 + k, X_BEFORE["lat"] + 4 * i + k + 1, 2048 + 1024 * i + k * T, G_ROW[name] + k)
            lo(U_CQ + 5, cols=8 * QH)
            with nc.vector.Fori(0, HEADS_C // 4) as it:
                for j in range(4):
                    lo(U_QKV + j + 2, it, 4, cols=UNIT)
            attention(HEADS_C, HEADS_A, True)
            dve.wait_ge(heads_ready, HEADS_BASE + HEADS_A + HEADS_C)
            k_major("o")
            turn_in("mlp1")
            mlp_up(1)
            k_major("dn1", skip_next=True)
            dve.wait_ge(rms2_ready, 2)
            for n in range(4):
                residual("final", n)
            dve.wait_ge(g_landed, 16)
            dve.wait_ge(rms_ready, 5)
            for t in range(TOK):
                nc.vector.scalar_tensor_tensor(final[:, t, :], h[:, t, :], rms[:, 4, t:t + 1], g_final,
                                               ALU.mult, ALU.mult).then_inc(final_ready, 1)

        @block.tensor
        def _(pe):
            def three(dst, x_hi, x_lo, wh, wl, first, last):
                nc.tensor.matmul(dst, x_hi, wh, start=first, stop=False)
                nc.tensor.matmul(dst, x_hi, wl, start=False, stop=False)
                return nc.tensor.matmul(dst, x_lo, wh, start=False, stop=last)

            def n_unit(u, ks, bank, first, last, it=None, per=0, cols=512):
                pe.wait_ge(lo_split, at(u + 1, it, per))
                s = u % SPLIT
                for i, k in enumerate(ks):
                    c = slice(i * cols, (i + 1) * cols)
                    for t in range(TOK):
                        b = 512 * (bank + t)
                        tok = slice(t * P, (t + 1) * P)
                        ins = three(ps[:, b:b + cols], xs[:, k, 0, tok], xs[:, k, 1, tok],
                                    w_hi[:, s, c], w_lo[:, s, c],
                                    first and i == 0, last and i == len(ks) - 1)
                ins.then_inc(unit_used, 1)

            def n_block(u, bank, it=None, per=0, between=None):
                for j in range(4):
                    n_unit(u + j, range(4 * j, 4 * j + 4), bank, j == 0, j == 3, it, per)
                    if between:
                        between(j)

            def k_major(name, banks_free):
                u0, k0, n = K_PHASES[name]

                def unit(j, first, last, it=None, free=None):
                    u = u0 + j
                    pe.wait_ge(jit_lo, at(k0 + j + 1, it, 4))
                    pe.wait_ge(lo_split, at(u + 1, it, 4))
                    for c in range(4):
                        if free and c in free:
                            free[c](pe)
                        for t in range(TOK):
                            b = 1024 * c + 512 * t
                            tok = slice(t * P, (t + 1) * P)
                            w = slice(512 * c, 512 * c + 512)
                            ins = three(ps[:, b:b + 512], js[:, j % SPLIT, 0, tok], js[:, j % SPLIT, 1, tok],
                                        w_hi[:, u % SPLIT, w], w_lo[:, u % SPLIT, w], first, last)
                        ins.then_inc(bank_pass if c < 3 else unit_used, 1)

                for j in range(4):
                    unit(j, j == 0, False, free=banks_free if j == 0 else None)
                with nc.tensor.Fori(0, n // 4 - 2) as it:
                    for j in range(4):
                        unit(4 + j, False, False, it)
                for j in range(n - 4, n):
                    unit(j, False, j == n - 1)

            def turn_block(n):
                for k in range(4):
                    for t in range(TOK):
                        c = 512 * n + 128 * k
                        b = 1024 * n + T * k + P * t
                        ins = nc.tensor.transpose(ps[:, b:b + P], h[:, t, c:c + P], ident[:, :])
                ins.then_inc(h_turned, 1)

            def turn_in(name):
                s = STAGES.index(name)
                for n in range(4):
                    if s:
                        pe.wait_ge(h_ready, 4 * (s - 1) + n + 1)
                    if s == 0 and n == 3:
                        pe.wait_ge(gains_ready, 1)
                    turn_block(n)

            def mlp_up(layer):
                u0, f0 = U_UP[layer], 16 * layer

                def turn(n, it=None):
                    pe.wait_ge(hid_ready, at(f0 + n + 1, it, 2))
                    for k in range(4):
                        for t in range(TOK):
                            b = 2048 + T * k + P * t
                            ins = nc.tensor.transpose(ps[:, b:b + P], hid[:, 512 * t + P * k:512 * t + P * k + P],
                                                      ident[:, :])
                    ins.then_inc(hid_turned, 1)

                def block_pair(n, it=None, first=False):
                    for a in range(2):
                        n_block(u0 + 4 * (n + a), 2 * a, it, 8,
                                lambda j: turn(n + a - 1, it) if j == 2 and not (first and a == 0) else None)

                block_pair(0, first=True)
                with nc.tensor.Fori(0, D_FF // 1024 - 1) as it:
                    block_pair(2, it)
                turn(D_FF // 512 - 1)

            def attention(n, h0, latent):
                q0, k0, u0, b0 = 0, 512, 512, 1024

                def turn(m, it=None):
                    pe.wait_ge(staged, at(h0 + m + 1, it, 2))
                    if h0 + m:
                        pe.wait_ge(turned_act, at(h0 + m, it, 2))
                        pe.wait_ge(turned_dve, at(h0 + m, it, 2))
                    s = 768 * (m % 2)
                    for t in range(TOK):
                        if latent:
                            q = s + QH * t
                            nc.tensor.transpose(ps[:, P * t:P * t + P], stage[:, q:q + P], ident[:, :])
                            k = s + 2 * QH + P * t
                            nc.tensor.transpose(ps[:, T + P * t:T + P * t + P], stage[:, k:k + P], ident[:, :])
                            ins = nc.tensor.transpose(ps[0:ROPE, 512 + P * t:512 + P * t + P],
                                                      stage[:, q + P:q + QH], ident[:, :])
                        else:
                            for i, b in enumerate((0, 512, 2560)):
                                src = stage[:, s + T * i + P * t:s + T * i + P * t + P]
                                ins = nc.tensor.transpose(ps[:, b + P * t:b + P * t + P], src, ident[:, :])
                    ins.then_inc(heads_turned, 1)

                def scores(m, it=None):
                    pe.wait_ge(turned_act, at(h0 + m + 1, it, 2))
                    if latent:
                        pe.wait_ge(turned_dve, at(h0 + m + 1, it, 2))
                    if h0 + m >= 2:
                        pe.wait_ge(exp_ready, at(h0 + m - 1, it, 2))
                    for q in range(2):
                        b = 1024 + 512 * (m % 2) + T * q
                        tok = slice(P * q, P * q + P)
                        if latent:
                            nc.tensor.matmul(ps[:, b:b + T], qT[:, tok], knT, start=True, stop=False)
                            ins = nc.tensor.matmul(ps[:, b:b + T], qrT[:, tok], krT[:, :], start=False, stop=True)
                        else:
                            kv = m // 4
                            if it is not None:
                                keys = kT[:, bass.ds(at(0, it, T), T)]
                            else:
                                keys = kT[:, T * kv:T * kv + T]
                            ins = nc.tensor.matmul(ps[:, b:b + T], qT[:, tok], keys, start=True, stop=True)
                    ins.then_inc(scores_ready, 1)

                def turn_probs(m, it=None):
                    pe.wait_ge(probs_ready, at(h0 + m + 1, it, 2))
                    if h0 + m:
                        pe.wait_ge(probT_ready, at(h0 + m, it, 2))
                    for k in range(2):
                        for q in range(2):
                            b = 2048 + T * k + P * q
                            src = prob[m % 2][:, T * q + P * k:T * q + P * k + P]
                            ins = nc.tensor.transpose(ps[:, b:b + P], src, ident[:, :])
                    ins.then_inc(probs_turned, 1)

                def values(m, it=None):
                    pe.wait_ge(probT_ready, at(h0 + m + 1, it, 2))
                    pe.wait_ge(v_staged, at(h0 + m + 1, it, 2))
                    pe.wait_ge(heads_ready, at(HEADS_BASE + h0 + m, it, 2))
                    for k in range(2):
                        v = 1536 + T * (m % 2) + P * k
                        ins = nc.tensor.matmul(ps[:, 3072:3328], stage[:, v:v + P], probT[:, T * k:T * k + T],
                                               start=(k == 0), stop=(k == 1))
                    ins.then_inc(heads_out, 1)

                for m, it in turns(nc.tensor, n):
                    if 0 <= m < n:
                        scores(m, it)
                    if 0 <= m + 1 < n:
                        turn(m + 1, it)
                    if 0 <= m - 2 < n:
                        values(m - 2, it)
                    if 0 <= m - 1 < n:
                        turn_probs(m - 1, it)

            pe.wait_ge(const_landed, 16 * 12)
            nc.tensor.transpose(ps[:, 3584:3584 + G_ROWS], gain_rows[:, :],
                                ident[0:G_ROWS, 0:G_ROWS]).then_inc(gains_turned, 1)
            pe.wait_ge(x_landed, 16 * TOK)
            turn_in("mix0")
            pe.wait_ge(xs_lo, KT)
            with nc.tensor.Fori(0, 3) as it:
                for b in range(3):
                    n_block(U_IN + 4 * b, 2 * b, it, 12)
            pe.wait_ge(qk_ready, 1)
            for g in range(KV_A):
                for t in range(TOK):
                    b = 3072 + T * g + P * t
                    c = HEADS_A * HD + HD * g
                    ins = nc.tensor.transpose(ps[:, b:b + P], projA[:, t, c:c + HD], ident[:, :])
            ins.then_inc(k_turned, 1)
            pe.wait_ge(mix_evac, IN_A // 512)
            pe.wait_ge(kT_ready, 1)
            attention(HEADS_A, 0, False)
            k_major("out", {0: lambda e: e.wait_ge(heads_ready, HEADS_BASE + HEADS_A)})
            turn_in("mlp0")
            pe.wait_ge(xs_lo, X_BEFORE["mlp0"] + KT)
            mlp_up(0)
            k_major("dn0", {2: lambda e: e.wait_ge(feat_ready, 16)})
            turn_in("mix1")
            pe.wait_ge(xs_lo, X_BEFORE["mix1"] + KT)
            pe.wait_ge(lo_split, U_KR + 1)
            s = U_KR % SPLIT
            for t in range(TOK):
                for k in range(KT):
                    tok, c, b = slice(t * P, (t + 1) * P), slice(ROPE * k, ROPE * k + ROPE), 512 * (6 + t)
                    ins = three(ps[:, b:b + ROPE], xs[:, k, 0, tok], xs[:, k, 1, tok],
                                w_hi[:, s, c], w_lo[:, s, c], k == 0, k == KT - 1)
            ins.then_inc(unit_used, 1)
            n_block(U_CKV, 0)
            n_block(U_CQ, 2)

            def turn_latent(which, bank):
                pe.wait_ge(lat_out, 2 - which)
                for k in range(4):
                    for t in range(TOK):
                        b = 512 * bank + T * k + P * t
                        ins = nc.tensor.transpose(ps[:, b:b + P], lat[:, which, t, P * k:P * k + P], ident[:, :])
                ins.then_inc(lat_turned, 1)

            turn_latent(1, 4)
            pe.wait_ge(kr_out, 1)
            turn_latent(0, 6)
            pe.wait_ge(kr_roped, 1)
            pe.wait_ge(lat_sq, 2)
            for t in range(TOK):
                ins = nc.tensor.transpose(ps[0:ROPE, P * t:P * t + P], kr[:, t, :], ident[:, :])
            ins.then_inc(kr_turned, 1)
            pe.wait_ge(krT_ready, 1)
            pe.wait_ge(xs_lo, X_BEFORE["lat"] + 8)
            with nc.tensor.Fori(0, HEADS_C // 4) as it:
                for a in range(2):
                    u = U_QKV + 2 * a
                    n_unit(u, range(4), 4 * a, True, True, it, 4)
                    n_unit(u + 1, range(4, 8), 4 * a + 2, True, True, it, 4, cols=2 * QH)
            pe.wait_ge(q_out, HEADS_C // 2)
            attention(HEADS_C, HEADS_A, True)
            k_major("o", {0: lambda e: e.wait_ge(heads_ready, HEADS_BASE + HEADS_A + HEADS_C)})
            turn_in("mlp1")
            pe.wait_ge(xs_lo, X_BEFORE["mlp1"] + KT)
            mlp_up(1)
            k_major("dn1", {2: lambda e: e.wait_ge(feat_ready, 32)})

        @block.gpsimd
        def _(pool):
            steps = [0]

            def step(ins):
                steps[0] += 1
                ins.then_inc(pool_step, 1)
                pool.wait_ge(pool_step, steps[0])

            def waited(it):
                if it is not None:
                    pool.sem_inc(pool_waited, 1)

            def inverse_rms(s):
                pool.wait_ge(squares, TOK * (s + 1))
                step(nc.gpsimd.tensor_scalar(meansq[:, s, :], sumsq[:, s, :], 1.0 / D, NORM_EPS,
                                             ALU.mult, ALU.add))
                nc.gpsimd.tensor_tensor(rms[:, s, :], meansq[:, s, :], half[:, 0:TOK],
                                        ALU.pow).then_inc(rms_ready, 1)
                if s in (1, 3):
                    pool.wait_ge(rms_ready, s + 1)
                    nc.gpsimd.tensor_tensor(rms2[:, s // 2, :], rms[:, s, :], rms[:, s, :],
                                            ALU.mult).then_inc(rms2_ready, 1)

            def attention(n, h0, latent):
                def stage_head(m, it=None):
                    if h0 + m >= 2:
                        pool.wait_ge(heads_turned, at(h0 + m - 1, it, 2))
                        waited(it)
                    s = 768 * (m % 2)
                    if latent:
                        nc.gpsimd.tensor_copy(stage[:, s:s + 2 * QH].rearrange("p (t c) -> p t c", t=2),
                                              qC[:, :, bass.ds(at(QH * m, it, 2 * QH), QH)])
                        nc.gpsimd.tensor_copy(stage[:, s + 2 * QH:s + 2 * QH + T]
                                              .rearrange("p (t c) -> p t c", t=2),
                                              kvC[:, :, bass.ds(at(2 * HD * m, it, 4 * HD), HD)]
                                              ).then_inc(staged, 1)
                    else:
                        def to(i):
                            return stage[:, s + T * i:s + T * i + T].rearrange("p (t c) -> p t c", t=2)

                        def of(c):
                            return projA[:, :, bass.ds(at(c + HD * m, it, 2 * HD), HD)]
                        nc.gpsimd.tensor_copy(to(0), of(0))
                        nc.gpsimd.tensor_tensor(to(1), of(C_AT), of(U_AT), ALU.mult)
                        nc.gpsimd.tensor_copy(to(2), of(B_AT)).then_inc(staged, 1)

                def stage_values(m, it=None):
                    if h0 + m >= 2:
                        pool.wait_ge(heads_out, at(h0 + m - 1, it, 2))
                        waited(it)
                    to = stage[:, 1536 + T * (m % 2):1536 + T * (m % 2) + T].rearrange("p (t c) -> p t c", t=2)
                    if latent:
                        src = kvC[:, :, bass.ds(at(2 * HD * m + HD, it, 4 * HD), HD)]
                    elif it is not None:
                        src = projA[:, :, bass.ds(at(QK_A, it, HD), HD)]
                    else:
                        src = projA[:, :, QK_A + HD * (m // 4):QK_A + HD * (m // 4) + HD]
                    nc.gpsimd.tensor_copy(to, src).then_inc(v_staged, 1)

                def gate(m, it=None):
                    y = feat[:, bass.ds(at((8 + m) * T, it, 2 * T), T)]
                    pool.wait_ge(taps, at(3 * m + 3, it, 6))
                    waited(it)
                    pool.wait_ge(turned_act, at(m + 1, it, 2))
                    waited(it)
                    nc.gpsimd.tensor_tensor(y, y, BT[m % 2], ALU.mult).then_inc(conv_ready, 1)

                stage_head(0)
                for m, it in turns(nc.gpsimd, n):
                    if 0 <= m + 2 < n and m >= -1:
                        stage_head(m + 2, it)
                    if 0 <= m < n:
                        stage_values(m, it)
                        if not latent:
                            gate(m, it)

            nc.gpsimd.memset(half[:, :], -0.5).then_inc(consts_set, 1)
            pool.wait_ge(consts_set, 2)
            inverse_rms(0)

            pool.wait_ge(mix_evac, 3)
            pool.wait_ge(const_landed, 16 * 12)
            x = projA[:, :, 0:QK_A].rearrange("p t (h c) -> p t h c", c=HD)
            sq = tmpA.rearrange("p (t h c) -> p t h c", t=TOK, c=HD)
            step(nc.gpsimd.tensor_tensor(sq, x, x, ALU.mult))
            w = HD // 2
            while w >= 1:
                step(nc.gpsimd.tensor_tensor(sq[:, :, :, 0:w], sq[:, :, :, 0:w], sq[:, :, :, w:2 * w], ALU.add))
                w //= 2
            step(nc.gpsimd.tensor_scalar(head_ms[:, :].rearrange("p (t h) -> p t h", t=TOK),
                                         sq[:, :, :, 0:1].rearrange("p t h o -> p t (h o)"),
                                         1.0 / HD, NORM_EPS, ALU.mult, ALU.add))
            step(nc.gpsimd.tensor_tensor(head_r[:, :, :].rearrange("p t h -> p (t h)"), head_ms[:, :],
                                         half[:, 0:20], ALU.pow))
            step(nc.gpsimd.tensor_scalar(head_r[:, :, 0:HEADS_A], head_r[:, :, 0:HEADS_A],
                                         float(HD) ** -0.5, None, ALU.mult))
            n_heads = HEADS_A + KV_A
            step(nc.gpsimd.tensor_tensor(x, x, head_r[:, :, :].unsqueeze(3).to_broadcast([P, TOK, n_heads, HD]),
                                         ALU.mult))
            for g, (a, b) in enumerate(((0, HEADS_A), (HEADS_A, n_heads))):
                gain = gqk[:, HD * g:HD * g + HD].unsqueeze(1).unsqueeze(1).to_broadcast([P, TOK, b - a, HD])
                step(nc.gpsimd.tensor_tensor(x[:, :, a:b, :], x[:, :, a:b, :], gain, ALU.mult))
            pairs = projA[:, :, 0:QK_A].rearrange("p t (h c two) -> p t h c two", c=HD // 2, two=2)
            hc = [P, TOK, n_heads, HD // 2]
            half_n = TOK * n_heads * HD // 2
            prod = [tmpA[:, 0:half_n], tmpA[:, half_n:2 * half_n], stage[:, 0:half_n], work[:, 0:half_n]]
            prod = [a.rearrange("p (t h c) -> p t h c", t=TOK, h=n_heads) for a in prod]
            cos, sin = (ropeA[:, i].unsqueeze(2).to_broadcast(hc) for i in range(2))
            even, odd = pairs[:, :, :, :, 0], pairs[:, :, :, :, 1]
            step(nc.gpsimd.tensor_tensor(prod[0], even, cos, ALU.mult))
            step(nc.gpsimd.tensor_tensor(prod[1], odd, sin, ALU.mult))
            step(nc.gpsimd.tensor_tensor(prod[2], even, sin, ALU.mult))
            step(nc.gpsimd.tensor_tensor(prod[3], odd, cos, ALU.mult))
            step(nc.gpsimd.tensor_tensor(even, prod[0], prod[1], ALU.subtract))
            step(nc.gpsimd.tensor_tensor(odd, prod[2], prod[3], ALU.add))
            nc.gpsimd.memset(head_ms[:, 0:1], 0.0).then_inc(qk_ready, 1)
            pool.wait_ge(mix_evac, IN_A // 512)
            attention(HEADS_A, 0, False)
            inverse_rms(1)
            inverse_rms(2)

            pool.wait_ge(kr_out, 1)
            krp = kr.rearrange("p t (c two) -> p t c two", two=2)
            cos_c, sin_c = rope_c[:, 0, :, :], rope_c[:, 1, :, :]
            for i, (part, f) in enumerate(((0, cos_c), (1, sin_c), (0, sin_c), (1, cos_c))):
                step(nc.gpsimd.tensor_tensor(kr_tmp[:, i], krp[:, :, :, part], f, ALU.mult))
            step(nc.gpsimd.tensor_tensor(krp[:, :, :, 0], kr_tmp[:, 0], kr_tmp[:, 1], ALU.subtract))
            nc.gpsimd.tensor_tensor(krp[:, :, :, 1], kr_tmp[:, 2], kr_tmp[:, 3], ALU.add).then_inc(kr_roped, 1)

            pool.wait_ge(lat_sq, 4)
            r = rms[:, 2, :]
            for w in range(2):
                step(nc.gpsimd.tensor_tensor(lat_t[:, 0, w, :], lat_ss[:, w, :], r, ALU.mult))
                step(nc.gpsimd.tensor_tensor(lat_t[:, 1, w, :], lat_t[:, 0, w, :], r, ALU.mult))
                step(nc.gpsimd.tensor_scalar(lat_t[:, 2, w, :], lat_t[:, 1, w, :], 1.0 / LORA, NORM_EPS,
                                             ALU.mult, ALU.add))
                step(nc.gpsimd.tensor_tensor(lat_t[:, 0, w, :], lat_t[:, 2, w, :], half[:, 0:TOK], ALU.pow))
                if w == 0:
                    step(nc.gpsimd.tensor_scalar(lat_t[:, 0, w, :], lat_t[:, 0, w, :], float(QH) ** -0.5,
                                                 None, ALU.mult))
                ins = nc.gpsimd.tensor_tensor(lat_s[:, w, :], lat_t[:, 0, w, :], r, ALU.mult)
                if w == 0:
                    step(ins)
            ins.then_inc(lat_scale, 1)

            tmp = [q_tmp[:, j, :].rearrange("p (t h c) -> p t h c", t=TOK, h=2) for j in range(4)]
            with nc.gpsimd.Fori(0, HEADS_C // 2) as it:
                pool.wait_ge(q_out, at(1, it, 1))
                waited(it)
                q = qC[:, :, bass.ds(at(0, it, 2 * QH), 2 * QH)].rearrange("p t (h c) -> p t h c", h=2)
                q = q[:, :, :, NOPE:QH].rearrange("p t h (c two) -> p t h c two", two=2)
                sh = [P, TOK, 2, ROPE // 2]
                c4, s4 = cos_c.unsqueeze(2).to_broadcast(sh), sin_c.unsqueeze(2).to_broadcast(sh)
                for i, (part, f) in enumerate(((0, c4), (1, s4), (0, s4), (1, c4))):
                    nc.gpsimd.tensor_tensor(tmp[i], q[:, :, :, :, part], f, ALU.mult).then_inc(q_prod, 1)
                pool.wait_ge(q_prod, at(4, it, 4))
                waited(it)
                nc.gpsimd.tensor_tensor(q[:, :, :, :, 0], tmp[0], tmp[1], ALU.subtract).then_inc(q_roped, 1)
                nc.gpsimd.tensor_tensor(q[:, :, :, :, 1], tmp[2], tmp[3], ALU.add).then_inc(q_roped, 1)
                pool.wait_ge(q_roped, at(2, it, 2))
            pool.wait_ge(kv_out, HEADS_C // 2)
            attention(HEADS_C, HEADS_A, True)
            inverse_rms(3)
            inverse_rms(4)


def turns(engine, n):
    for m in (-1, 0, 1):
        yield m, None
    with engine.Fori(0, (n - 4) // 2) as it:
        for m in (2, 3):
            yield m, it
    for m in range(n - 2, n + 2):
        yield m, None


_INS = ["x", "even_norm_g", "even_w_in", "even_q_norm_g", "even_k_norm_g", "even_conv_w", "even_w_out",
        "odd_norm_g", "odd_w_down", "odd_q_lat_g", "odd_kv_lat_g", "odd_w_uq", "odd_w_ukv", "odd_w_o",
        "mlp_norm_g", "mlp_w_up", "mlp_w_down", "final_norm_g"]


def _rope_table(np, rot_dim, grid_w=64):
    t = np.arange(T)
    axis = rot_dim // 2
    exponent = -np.arange(0, axis, 2, dtype=np.float32) / np.float32(axis)
    inv = np.power(np.float32(10000.0), exponent, dtype=np.float32)
    row, col = (t // grid_w).astype(np.float32), (t % grid_w).astype(np.float32)
    ang = np.concatenate([row[:, None] * inv, col[:, None] * inv], axis=-1)
    both = np.stack([np.cos(ang), np.sin(ang)]).astype(np.float32)
    return np.ascontiguousarray(both.reshape(2, TOK, P, -1).transpose(2, 0, 1, 3))


def kernel(**inputs):
    import numpy as _np
    import concourse.bacc as _bacc
    from concourse import mybir as _mybir
    from concourse.bass_utils import run_bass_kernel_spmd as _run

    nc = _bacc.Bacc("TRN2", target_bir_lowering=False, num_devices=1, dynamic_dma_scratch_size=1024)
    arrays, args = {}, {}

    def give(name, a):
        a = _np.ascontiguousarray(a)
        arrays[f"in_{name}_dram"] = a
        args[name] = nc.dram_tensor(f"in_{name}_dram", a.shape, _mybir.dt.from_np(a.dtype),
                                    kind="ExternalInput").ap()

    for name in _INS:
        give(name, inputs[name])
    give("ident", _np.eye(P, dtype=_np.float32))
    give("rope_a", _rope_table(_np, HD))
    give("rope_c", _rope_table(_np, ROPE))
    out = nc.dram_tensor("out_0_dram", (1, T, D), F32, kind="ExternalOutput").ap()
    build(nc, args, out)
    r = _run(nc, [arrays], core_ids=[0])
    return r.results[0]["out_0_dram"]
```

```python
from contextlib import ExitStack

import concourse.bass as bass
from concourse import mybir
from concourse.alu_op_type import AluOpType as ALU

ACT = mybir.ActivationFunctionType
F32 = mybir.dt.float32
F32R = mybir.dt.float32r
BF16 = mybir.dt.bfloat16
AX_X = mybir.AxisListType.X

P = 128
D = 2048
TOK = 2
T = TOK * P
KT = D // P
NORM_EPS = 1e-6

HEADS_A, KV_A, HD = 8, 2, 128
QK_A = (HEADS_A + KV_A) * HD
IN_A = 4608
B_AT, C_AT, U_AT = 1536, 2560, 3584
HEADS_C, NOPE, ROPE = 16, 128, 64
QH = NOPE + ROPE
LORA = 512
D_FF = 8192

UNIT = 2048
RAW = 4
SPLIT = 2

U_IN = 0
U_OUT = U_IN + 4 * (IN_A // 512)
U_UP = [0, 0]
U_DN = [0, 0]
U_UP[0] = U_OUT + KT
U_DN[0] = U_UP[0] + 4 * (D_FF // 512)
U_CKV = U_DN[0] + D_FF // P
U_KR = U_CKV + 4
U_CQ = U_KR + 1
U_QKV = U_CQ + 4
U_O = U_QKV + HEADS_C
U_UP[1] = U_O + KT
U_DN[1] = U_UP[1] + 4 * (D_FF // 512)
U_END = U_DN[1] + D_FF // P

K_OUT, K_DN0, K_O, K_DN1 = 0, KT, KT + D_FF // P, 2 * KT + D_FF // P

X_BEFORE = {"mix0": 0, "mlp0": 16, "mix1": 32, "lat": 48, "mlp1": 56}
STAGES = ["mix0", "mlp0", "mix1", "mlp1", "final"]

G_ROW = {"mix0": 0, "mlp0": 16, "mix1": 32, "mlp1": 48, "q_lat": 64, "kv_lat": 68, "taps": 72}
G_ROWS = 96


HEADS_BASE = 1


def at(c, it=None, per=0):
    return c if it is None else it * per + c


def landed_count(u, it=None, per=0):
    return at(16 * (u // RAW + 1), it, 16 * per // RAW)


def build(nc, A, out):
    ctx = ExitStack()
    with ctx:
        def sb(name, shape, dt=F32):
            return ctx.enter_context(nc.sbuf_tensor(name, shape, dt))

        def sem(name):
            return ctx.enter_context(nc.semaphore(name))

        ps = ctx.enter_context(nc.psum_tensor("ps", [P, 8 * 512], F32))
        h = sb("h", [P, TOK, D])
        xs = sb("xs", [P, KT, 2, T], F32R)
        raw = sb("raw", [P, RAW, UNIT])
        w_hi = sb("w_hi", [P, SPLIT, UNIT], F32R)
        w_lo = sb("w_lo", [P, SPLIT, UNIT], F32R)
        js = sb("js", [P, SPLIT, 2, T], F32R)
        big = sb("big", [P, 18432])
        work = sb("work", [P, 3072])
        stage = sb("stage", [P, 2048])
        ident = sb("ident", [P, P])
        gain_rows = sb("gain_rows", [G_ROWS, P])
        gains = sb("gains", [P, G_ROWS])
        rope_c = sb("rope_c", [P, 2, TOK, ROPE // 2])
        krT = sb("krT", [ROPE, T])
        sumsq = sb("sumsq", [P, 5, TOK])
        sumsq_part = sb("sumsq_part", [P, TOK, 4])
        meansq = sb("meansq", [P, 5, TOK])
        rms = sb("rms", [P, 5, TOK])
        rms2 = sb("rms2", [P, 2, TOK])
        half = sb("half", [P, 24])
        lat_ss = sb("lat_ss", [P, 2, TOK])
        lat_t = sb("lat_t", [P, 3, 2, TOK])
        lat_s = sb("lat_s", [P, 2, TOK])
        head_ms = sb("head_ms", [P, 2 * 10])
        head_r = sb("head_r", [P, 2, 10])
        nmax = sb("nmax", [P, 2, 2])
        rsum = sb("rsum", [P, 2, 2])
        rrec = sb("rrec", [P, 2, 2])

        feat = big[:, 0:64 * T]
        projA = big[:, 4096:4096 + 2 * IN_A].rearrange("p (t c) -> p t c", t=TOK)
        tmpA = big[:, 13312:13312 + 2 * QK_A]
        kT = big[:, 15872:15872 + KV_A * T]
        ropeA = big[:, 16384:16640].rearrange("p (s t c) -> p s t c", s=2, t=TOK)
        gqk = big[:, 16640:16896]
        lat = big[:, 0:2048].rearrange("p (w t c) -> p w t c", w=2, t=TOK)
        kr = big[:, 2048:2176].rearrange("p (t c) -> p t c", t=TOK)
        kr_tmp = big[:, 2176:2432].rearrange("p (j t c) -> p j t c", j=4, t=TOK)
        q_tmp = big[:, 2432:2944].rearrange("p (j c) -> p j c", j=4)
        qC = big[:, 4096:4096 + 2 * 3072].rearrange("p (t c) -> p t c", t=TOK)
        kvC = big[:, 10240:10240 + 2 * 4096].rearrange("p (t c) -> p t c", t=TOK)
        g_final = big[:, 16384:18432]
        final = big[:, 0:2 * D].rearrange("p (t c) -> p t c", t=TOK)

        relu_z, hid = work[:, 0:1024], work[:, 1024:2048]
        qT, knT, qrT = work[:, 0:256], work[:, 256:512], work[0:ROPE, 2560:2816]
        prob = [work[:, 512 + 512 * i:1024 + 512 * i] for i in range(2)]
        probT = work[:, 1536:2048]
        BT = [work[:, 2048 + 256 * i:2304 + 256 * i] for i in range(2)]
        cuT = sb("cuT", [P, 2, T + 2])

        raw_landed = [sem(f"raw_landed{i}") for i in range(RAW)]
        const_landed, g_landed = sem("const_landed"), sem("g_landed")
        hi_split, lo_split, unit_used = sem("hi_split"), sem("lo_split"), sem("unit_used")
        jit_hi, jit_lo = sem("jit_hi"), sem("jit_lo")
        bank_pass = sem("bank_pass")
        gains_turned, gains_ready = sem("gains_turned"), sem("gains_ready")
        consts_set = sem("consts_set")
        h_ready, h_turned = sem("h_ready"), sem("h_turned")
        xs_hi, xs_lo = sem("xs_hi"), sem("xs_lo")
        kv_half = sem("kv_half")
        squares, part_squares, rms_ready = sem("squares"), sem("part_squares"), sem("rms_ready")
        rms2_ready = sem("rms2_ready")
        mix_evac = sem("mix_evac")
        pool_step = sem("pool_step")
        qk_ready = sem("qk_ready")
        k_turned, kT_ready = sem("k_turned"), sem("kT_ready")
        staged, gate_staged, v_staged = sem("staged"), sem("gate_staged"), sem("v_staged")
        heads_turned, turned_act, turned_dve = sem("heads_turned"), sem("turned_act"), sem("turned_dve")
        scores_ready, max_ready, exp_ready = sem("scores_ready"), sem("max_ready"), sem("exp_ready")
        recip_ready, probs_ready = sem("recip_ready"), sem("probs_ready")
        probs_turned, probT_ready = sem("probs_turned"), sem("probT_ready")
        heads_out, heads_ready = sem("heads_out"), sem("heads_ready")
        taps, conv_ready = sem("taps"), sem("conv_ready")
        relu_ready, hid_ready = sem("relu_ready"), sem("hid_ready")
        hid_turned, feat_ready = sem("hid_turned"), sem("feat_ready")
        kr_out, kr_roped, kr_turned, krT_ready = sem("kr_out"), sem("kr_roped"), sem("kr_turned"), sem("krT_ready")
        lat_out, lat_sq, lat_turned, lat_scale = sem("lat_out"), sem("lat_sq"), sem("lat_turned"), sem("lat_scale")
        kv_out, q_out, q_prod, q_roped = sem("kv_out"), sem("q_out"), sem("q_prod"), sem("q_roped")
        pool_waited, act_waited = sem("pool_waited"), sem("act_waited")
        final_ready, stored = sem("final_ready"), sem("stored")
        x_landed = [sem(f"x_landed{n}") for n in range(4)]
        rope_landed = sem("rope_landed")

        block = ctx.enter_context(nc.Block())

        K_PHASES = {"out": (U_OUT, K_OUT, KT), "dn0": (U_DN[0], K_DN0, D_FF // P),
                    "o": (U_O, K_O, KT), "dn1": (U_DN[1], K_DN1, D_FF // P)}
        AFTER = {"mlp0": "out", "mix1": "dn0", "mlp1": "o", "final": "dn1"}
        NEXT = {product: stage for stage, product in AFTER.items()}

        def proj_bank(b):
            return 0 if b == 0 else 2 if b % 2 else 6

        FIRST_UNIT = {"mix0": U_IN, "mlp0": U_UP[0], "mix1": U_CKV, "mlp1": U_UP[1]}

        @block.sync
        def _(sp):
            def load(u, src, cols, it=None, per=0):
                if u >= RAW:
                    sp.wait_ge(lo_split, at(u - RAW + 1, it, per))
                s = u % RAW
                dst = raw[:, s, 0:cols]
                if len(src.shape) == 3:
                    dst = dst.rearrange("p (k c) -> p k c", k=src.shape[1])
                sp.dma_start(dst, src).then_inc(raw_landed[s], 16)

            def tiles(w):
                return w.rearrange("(k p) c -> p k c", p=P)

            w = tiles(A["even_w_in"][0])
            x = A["x"][0].rearrange("(t p) c -> p t c", p=P)

            def load_x(n):
                sp.dma_start(h[:, :, 512 * n:512 * n + 512], x[:, :, 512 * n:512 * n + 512]
                             ).then_inc(x_landed[n], 16)

            load_x(0)
            for j in range(RAW):
                load(U_IN + j, w[:, 4 * j:4 * j + 4, 0:512], UNIT)
                if j == 0:
                    for n in range(1, 4):
                        load_x(n)
            sp.dma_start(ropeA, A["rope_a"]).then_inc(rope_landed, 16)
            sp.dma_start(rope_c[:, :, :, :], A["rope_c"]).then_inc(rope_landed, 16)
            sp.dma_start(gqk[:, 0:HD], A["even_q_norm_g"].to_broadcast([P, HD])).then_inc(rope_landed, 16)
            sp.dma_start(gqk[:, HD:2 * HD], A["even_k_norm_g"].to_broadcast([P, HD])).then_inc(rope_landed, 16)
            with nc.sync.Fori(0, IN_A // 512 - 1) as it:
                for j in range(4):
                    load(U_IN + 4 + j, w[:, 4 * j:4 * j + 4, bass.ds(at(512, it, 512), 512)], UNIT, it, 4)

            def k_major(w, u0, n):
                w = w.rearrange("(g k p) c -> p g k c", p=P, k=4)
                with nc.sync.Fori(0, n // 4) as it:
                    for j in range(4):
                        load(u0 + j, w[:, bass.ds(it, 1), j, :].rearrange("p g c -> p (g c)"), UNIT, it, 4)

            def n_major(w, u0, blocks):
                w = tiles(w)
                with nc.sync.Fori(0, blocks) as it:
                    for j in range(4):
                        load(u0 + j, w[:, 4 * j:4 * j + 4, bass.ds(at(0, it, 512), 512)], UNIT, it, 4)

            k_major(A["even_w_out"][0], U_OUT, KT)
            n_major(A["mlp_w_up"][0], U_UP[0], D_FF // 512)
            k_major(A["mlp_w_down"][0], U_DN[0], D_FF // P)
            w = tiles(A["odd_w_down"][0])
            for j in range(4):
                load(U_CKV + j, w[:, 4 * j:4 * j + 4, LORA:2 * LORA], UNIT)
            load(U_KR, w[:, :, 2 * LORA:2 * LORA + ROPE], KT * ROPE)
            for j in range(4):
                load(U_CQ + j, w[:, 4 * j:4 * j + 4, 0:LORA], UNIT)
            wq, wkv = tiles(A["odd_w_uq"][0]), tiles(A["odd_w_ukv"][0])
            with nc.sync.Fori(0, HEADS_C // 4) as it:
                for a in range(2):
                    load(U_QKV + 2 * a, wkv[:, :, bass.ds(at(512 * a, it, 1024), 512)], UNIT, it, 4)
                    load(U_QKV + 2 * a + 1, wq[:, :, bass.ds(at(2 * QH * a, it, 4 * QH), 2 * QH)],
                         8 * QH, it, 4)
            k_major(A["odd_w_o"][0], U_O, KT)
            sp.wait_ge(heads_ready, HEADS_BASE + HEADS_A + HEADS_C)
            sp.dma_start(g_final, A["final_norm_g"].rearrange("(a c) -> a c", a=1)
                         .to_broadcast([P, D])).then_inc(g_landed, 16)
            n_major(A["mlp_w_up"][1], U_UP[1], D_FF // 512)
            k_major(A["mlp_w_down"][1], U_DN[1], D_FF // P)
            for i in range(4):
                t, c = i // 2, slice(D // 2 * (i % 2), D // 2 * (i % 2 + 1))
                sp.wait_ge(final_ready, i + 1)
                sp.dma_start(out[0, t * P:(t + 1) * P, c], final[:, t, c]).then_inc(stored, 16)
            sp.wait_ge(stored, 16 * 4)

        @block.scalar
        def _(act):
            act.dma_start(ident[:, :], A["ident"]).then_inc(const_landed, 16)
            act.dma_start(gain_rows[:, :], A["gain_rows"]).then_inc(const_landed, 16)

            def hi(u, it=None, per=0, cols=UNIT):
                act.wait_ge(raw_landed[u % RAW], landed_count(u, it, per))
                if u >= SPLIT:
                    act.wait_ge(unit_used, at(u - SPLIT + 1, it, per))
                nc.scalar.activation(w_hi[:, u % SPLIT, 0:cols], raw[:, u % RAW, 0:cols],
                                     ACT.Copy).then_inc(hi_split, 1)

            def hi_kv(u, it=None, per=0):
                act.wait_ge(raw_landed[u % RAW], landed_count(u, it, per))
                act.wait_ge(unit_used, at(u - SPLIT + 1, it, per))
                for i, done in enumerate((kv_half, hi_split)):
                    c = slice(UNIT // 2 * i, UNIT // 2 * (i + 1))
                    nc.scalar.activation(w_hi[:, u % SPLIT, c], raw[:, u % RAW, c], ACT.Copy).then_inc(done, 1)

            def turn_in(name):
                s, u0 = STAGES.index(name), FIRST_UNIT[name]

                def high(n):
                    act.wait_ge(h_turned, 4 * s + n + 1)
                    for k in range(4 * n, 4 * n + 4):
                        nc.scalar.activation(xs[:, k, 0, :], ps[:, k * T:(k + 1) * T], ACT.Copy,
                                             scale=gains[:, G_ROW[name] + k:G_ROW[name] + k + 1]
                                             ).then_inc(xs_hi, 1)

                if name == "mix0":
                    hi(u0)
                high(0)
                high(1)
                hi(u0 + 1)
                high(2)
                hi(u0 + 2)
                square(s, 0)
                high(3)
                hi(u0 + 3)
                square(s, 1)
                hi(u0 + 4, cols=KT * ROPE if u0 + 4 == U_KR else UNIT)
                act.wait_ge(squares, TOK * s + TOK)

            def waited(it):
                if it is not None:
                    act.sem_inc(act_waited, 1)

            def square(s, t):
                if s:
                    act.wait_ge(h_ready, 4 * s)
                else:
                    for n in range(4):
                        act.wait_ge(x_landed[n], 16)
                if s or t:
                    act.wait_ge(squares, TOK * s + t)
                nc.scalar.activation(work[:, 0:D], h[:, t, :], ACT.Square,
                                     accum_out=sumsq[:, s, t:t + 1]).then_inc(squares, 1)

            def jit(name, k, it=None):
                u0, k0, n = K_PHASES[name]
                if k >= SPLIT:
                    act.wait_ge(unit_used, at(u0 + k - SPLIT + 1, it, 4))
                nc.scalar.activation(js[:, k % SPLIT, 0, :], feat[:, bass.ds(at(k * T, it, 4 * T), T)],
                                     ACT.Copy).then_inc(jit_hi, 1)

            def k_major(name, skip_next=False):
                u0, k0, n = K_PHASES[name]
                with nc.scalar.Fori(0, n // 4 - 1) as it:
                    for j in range(4):
                        jit(name, j + 2, it)
                        hi(u0 + j + 2, it, 4)
                for j in range(n - 4, n):
                    if j + 2 < n:
                        jit(name, j + 2)
                        hi(u0 + j + 2)
                    elif j + 2 == n and not skip_next:
                        hi(u0 + n)

            def attention(n, h0, latent, last_out):
                name, u_next = ("o", U_O) if latent else ("out", U_OUT)

                def copies(m, it=None):
                    act.wait_ge(heads_turned, at(h0 + m + 1, it, 2))
                    if latent:
                        nc.scalar.activation(work[:, 0:512], ps[:, 0:512], ACT.Copy).then_inc(turned_act, 1)
                    else:
                        nc.scalar.activation(qT, ps[:, 0:256], ACT.Copy)
                        if m >= 2:
                            act.wait_ge(conv_ready, at(m - 1, it, 2))
                        nc.scalar.activation(BT[m % 2], ps[:, 2560:2816], ACT.Copy).then_inc(turned_act, 1)

                def stage_gate(m, it=None):
                    if m >= 2:
                        act.wait_ge(heads_turned, at(m - 1, it, 2))
                        waited(it)
                    s = 768 * (m % 2) + 2 * T
                    nc.scalar.activation(stage[:, s:s + T].rearrange("p (t c) -> p t c", t=2),
                                         projA[:, :, bass.ds(at(B_AT + HD * m, it, 2 * HD), HD)],
                                         ACT.Copy).then_inc(gate_staged, 1)

                def stage_values(m, it=None):
                    if m >= 2:
                        act.wait_ge(heads_out, at(m - 1, it, 2))
                        waited(it)
                    s = 1536 + T * (m % 2)
                    if it is not None:
                        src = projA[:, :, bass.ds(at(QK_A, it, HD), HD)]
                    else:
                        src = projA[:, :, QK_A + HD * (m // 4):QK_A + HD * (m // 4) + HD]
                    nc.scalar.activation(stage[:, s:s + T].rearrange("p (t c) -> p t c", t=2), src,
                                         ACT.Copy).then_inc(v_staged, 1)

                def exps(m, it=None):
                    act.wait_ge(max_ready, at(h0 + m + 1, it, 2))
                    if h0 + m >= 2:
                        act.wait_ge(probs_turned, at(h0 + m - 1, it, 2))
                    b = 1024 + 512 * (m % 2)
                    for q in range(2):
                        ins = nc.scalar.activation(prob[m % 2][:, q * T:(q + 1) * T],
                                                   ps[:, b + q * T:b + (q + 1) * T], ACT.Exp,
                                                   bias=nmax[:, m % 2, q:q + 1],
                                                   accum_out=rsum[:, m % 2, q:q + 1])
                    ins.then_inc(exp_ready, 1)

                def turned(m, it=None):
                    act.wait_ge(probs_turned, at(h0 + m + 1, it, 2))
                    nc.scalar.activation(probT, ps[:, 2048:2560], ACT.Copy).then_inc(probT_ready, 1)

                if not latent:
                    stage_gate(0)
                for m, it in turns(nc.scalar, n):
                    if 0 <= m + 1 < n:
                        copies(m + 1, it)
                    if not latent and m + 2 < n:
                        stage_gate(m + 2, it)
                    if 0 <= m < n:
                        exps(m, it)
                        if not latent:
                            stage_values(m, it)
                    if m == -1:
                        last_out()
                    if m == n - 2:
                        act.wait_ge(heads_ready, HEADS_BASE + h0 + 2)
                        jit(name, 0)
                        jit(name, 1)
                    if 0 <= m - 1 < n:
                        turned(m - 1, it)
                hi(u_next + 1)

            def mlp_up(layer):
                u0, f0 = U_UP[layer], 16 * layer

                def move(n, it=None):
                    act.wait_ge(hid_turned, at(f0 + n + 1, it, 2))
                    nc.scalar.activation(feat[:, bass.ds(at(n * 4 * T, it, 8 * T), 4 * T)],
                                         ps[:, 2048:3072], ACT.Copy).then_inc(feat_ready, 1)

                dn = "dn%d" % layer

                def relu(n, it=None):
                    a = n % 2
                    act.wait_ge(unit_used, at(u0 + 4 * n + 4, it, 8))
                    nc.scalar.activation(relu_z, ps[:, 1024 * a:1024 * a + 1024],
                                         ACT.Relu).then_inc(relu_ready, 1)

                def block(n, it=None, last=False):
                    u = u0 + 4 * n
                    if n:
                        for j in range(3):
                            hi(u + j + 2, it, 8)
                        move(n - 1, it)
                    if last:
                        act.wait_ge(feat_ready, f0 + 1)
                        jit(dn, 0)
                        relu(n)
                        hi(u + 5)
                        jit(dn, 1)
                        move(n)
                    else:
                        hi(u + 5, it, 8)
                        relu(n, it)

                n = D_FF // 512
                block(0)
                block(1)
                with nc.scalar.Fori(0, n // 2 - 2) as it:
                    block(2, it)
                    block(3, it)
                block(n - 2)
                block(n - 1, last=True)

            act.wait_ge(gains_turned, 1)
            nc.scalar.activation(gains[:, :], ps[:, 3584:3584 + G_ROWS], ACT.Copy).then_inc(gains_ready, 1)
            act.wait_ge(gains_ready, 1)
            turn_in("mix0")
            act.wait_ge(rms_ready, 1)

            def project(b, it=None):
                act.wait_ge(unit_used, at(U_IN + 4 * b + 4, it, 8))
                for t in range(TOK):
                    z = 512 * (proj_bank(b) + t)
                    ins = nc.scalar.activation(projA[:, t, bass.ds(at(512 * b, it, 1024), 512)],
                                               ps[:, z:z + 512], ACT.Copy, scale=rms[:, 0, t:t + 1])
                ins.then_inc(mix_evac, 1)

            hi(U_IN + 5)
            project(0)
            last = IN_A // 512 - 1
            with nc.scalar.Fori(0, last // 2 - 1) as it:
                for b in (1, 2):
                    for j in range(4):
                        hi(U_IN + 4 * b + j + 2, it, 8)
                    project(b, it)
            for j in range(4):
                hi(U_IN + 4 * last + j - 2)
            project(last - 1)
            hi(U_IN + 4 * last + 2)
            hi(U_IN + 4 * last + 3)
            act.wait_ge(k_turned, 1)
            nc.scalar.activation(kT, ps[:, 2048:2560], ACT.Copy).then_inc(kT_ready, 1)
            hi(U_OUT)
            attention(HEADS_A, 0, False, lambda: project(last))

            act.wait_ge(heads_ready, HEADS_BASE + HEADS_A)
            act.wait_ge(conv_ready, HEADS_A)
            k_major("out")
            turn_in("mlp0")
            mlp_up(0)
            act.wait_ge(feat_ready, 16)
            k_major("dn0")
            turn_in("mix1")

            def latent_out(which, bank):
                nc.scalar.activation(lat[:, which, :, :].rearrange("p t c -> p (t c)"),
                                     ps[:, 512 * bank:512 * bank + 1024], ACT.Copy).then_inc(lat_out, 1)
                for t in range(TOK):
                    if which == 0 or t:
                        act.wait_ge(lat_sq, (2 if which == 0 else 0) + t)
                    nc.scalar.activation(work[:, 0:512], ps[:, 512 * (bank + t):512 * (bank + t) + 512],
                                         ACT.Square, accum_out=lat_ss[:, which, t:t + 1]).then_inc(lat_sq, 1)

            hi(U_CQ)
            act.wait_ge(unit_used, U_CKV + 4)
            latent_out(1, 0)
            hi(U_CQ + 1)
            act.wait_ge(unit_used, U_KR + 1)
            act.wait_ge(rms_ready, 3)
            for t in range(TOK):
                ins = nc.scalar.activation(kr[:, t, :], ps[:, 512 * (6 + t):512 * (6 + t) + ROPE], ACT.Copy,
                                           scale=rms[:, 2, t:t + 1])
            ins.then_inc(kr_out, 1)
            hi(U_CQ + 2)
            hi(U_CQ + 3)

            def latent_high(which, name, k0):
                act.wait_ge(lat_turned, 2 - which)
                for k in range(4):
                    b = 2048 + 1024 * (1 - which) + k * T
                    nc.scalar.activation(xs[:, k0 + k, 0, :], ps[:, b:b + T], ACT.Copy,
                                         scale=gains[:, G_ROW[name] + k:G_ROW[name] + k + 1]
                                         ).then_inc(xs_hi, 1)

            latent_high(1, "kv_lat", 0)
            hi(U_QKV)
            act.wait_ge(kr_turned, 1)
            nc.scalar.activation(krT[:, :], ps[0:ROPE, 0:T], ACT.Copy).then_inc(krT_ready, 1)
            act.wait_ge(unit_used, U_CQ + 4)
            latent_out(0, 2)
            hi(U_QKV + 1, cols=8 * QH)
            latent_high(0, "q_lat", 4)
            act.wait_ge(lat_scale, 1)

            def pair_out(a, q, it=None):
                act.wait_ge(unit_used, at(U_QKV + 2 * a + q + 1, it, 4))
                for t in range(TOK):
                    b = 2048 * (a % 2) + 1024 * q + 512 * t
                    if q:
                        dst = qC[:, t, bass.ds(at(2 * QH * a, it, 4 * QH), 2 * QH)]
                        ins = nc.scalar.activation(dst, ps[:, b:b + 2 * QH], ACT.Copy,
                                                   scale=lat_s[:, 0, t:t + 1])
                    else:
                        dst = kvC[:, t, bass.ds(at(512 * a, it, 1024), 512)]
                        ins = nc.scalar.activation(dst, ps[:, b:b + 512], ACT.Copy,
                                                   scale=lat_s[:, 1, t:t + 1])
                ins.then_inc(q_out if q else kv_out, 1)

            pairs = HEADS_C // 2
            with nc.scalar.Fori(0, pairs // 2 - 1) as it:
                for a in range(2):
                    hi_kv(U_QKV + 2 * a + 2, it, 4)
                    pair_out(a, 0, it)
                    hi(U_QKV + 2 * a + 3, it, 4, cols=8 * QH)
                    pair_out(a, 1, it)
            hi_kv(U_O - 2)
            pair_out(pairs - 2, 0)
            hi(U_O - 1, cols=8 * QH)
            pair_out(pairs - 2, 1)
            hi(U_O)
            pair_out(pairs - 1, 0)
            attention(HEADS_C, HEADS_A, True, lambda: pair_out(pairs - 1, 1))
            act.wait_ge(heads_ready, HEADS_BASE + HEADS_A + HEADS_C)
            k_major("o")
            turn_in("mlp1")
            mlp_up(1)
            act.wait_ge(feat_ready, 32)
            k_major("dn1", skip_next=True)
            for n in range(4):
                act.wait_ge(h_ready, 12 + n + 1)
                for t in range(TOK):
                    i = TOK * n + t
                    nc.scalar.activation(work[:, 256 * i:256 * i + 256].bitcast(BF16), h[:, t, 512 * n:512 * n + 512],
                                         ACT.Square, accum_out=sumsq_part[:, t, n:n + 1]).then_inc(part_squares, 1)

        @block.vector
        def _(dve):
            def lo(u, it=None, per=0, cols=UNIT):
                dve.wait_ge(hi_split, at(u + 1, it, per))
                nc.vector.tensor_tensor(w_lo[:, u % SPLIT, 0:cols], raw[:, u % RAW, 0:cols],
                                        w_hi[:, u % SPLIT, 0:cols].bitcast(F32),
                                        ALU.subtract).then_inc(lo_split, 1)

            def lo_kv(u, it=None, per=0):
                halves = (u - U_QKV) // 2
                for i in range(2):
                    c = slice(UNIT // 2 * i, UNIT // 2 * (i + 1))
                    if i == 0:
                        dve.wait_ge(kv_half, at(halves, it, per // 2))
                    else:
                        dve.wait_ge(hi_split, at(u + 1, it, per))
                    ins = nc.vector.tensor_tensor(w_lo[:, u % SPLIT, c], raw[:, u % RAW, c],
                                                  w_hi[:, u % SPLIT, c].bitcast(F32), ALU.subtract)
                ins.then_inc(lo_split, 1)

            def xs_low(k, x_count, b, g):
                dve.wait_ge(xs_hi, x_count + (k + 1) % 2)
                nc.vector.scalar_tensor_tensor(xs[:, k, 1, :], ps[:, b:b + T], gains[:, g:g + 1],
                                               xs[:, k, 0, :].bitcast(F32), ALU.mult,
                                               ALU.subtract).then_inc(xs_lo, 1)

            def residual(name, n):
                s = STAGES.index(name)
                u0, k0, count = K_PHASES[AFTER[name]]
                if n < 3:
                    dve.wait_ge(bank_pass, 3 * (k0 + count - 1) + n + 1)
                else:
                    dve.wait_ge(unit_used, u0 + count)
                for t in range(TOK):
                    b, to = 1024 * n + 512 * t, h[:, t, 512 * n:512 * n + 512]
                    if name in ("mix1", "final"):
                        ins = nc.vector.scalar_tensor_tensor(to, ps[:, b:b + 512],
                                                             rms2[:, s // 4, t:t + 1], to,
                                                             ALU.mult, ALU.add)
                    else:
                        ins = nc.vector.tensor_tensor(to, ps[:, b:b + 512], to, ALU.add)
                ins.then_inc(h_ready, 1)

            def turn_in(name):
                u0, first = FIRST_UNIT[name], name == "mix0"

                def low(n):
                    for k in range(4 * n, 4 * n + 4):
                        xs_low(k, X_BEFORE[name] + k + 1, k * T, G_ROW[name] + k)
                if name == "mix1":
                    dve.wait_ge(rms2_ready, 1)
                if not first:
                    residual(name, 0)
                    residual(name, 1)
                lo(u0)
                low(0)
                if not first:
                    residual(name, 2)
                low(1)
                lo(u0 + 1)
                if not first:
                    residual(name, 3)
                low(2)
                lo(u0 + 2)
                low(3)
                lo(u0 + 3)
                lo(u0 + 4, cols=KT * ROPE if u0 + 4 == U_KR else UNIT)

            def jit(name, k, it=None):
                dve.wait_ge(jit_hi, at(K_PHASES[name][1] + k + 1, it, 4))
                nc.vector.tensor_tensor(js[:, k % SPLIT, 1, :], feat[:, bass.ds(at(k * T, it, 4 * T), T)],
                                        js[:, k % SPLIT, 0, :].bitcast(F32),
                                        ALU.subtract).then_inc(jit_lo, 1)

            def k_major(name):
                u0, k0, n = K_PHASES[name]
                with nc.vector.Fori(0, n // 4 - 1) as it:
                    for j in range(4):
                        jit(name, j + 2, it)
                        lo(u0 + j + 2, it, 4)
                for j in range(n - 4, n):
                    if j + 2 < n:
                        jit(name, j + 2)
                        lo(u0 + j + 2)

            def mlp_up(layer):
                u0, f0, dn = U_UP[layer], 16 * layer, "dn%d" % layer

                def square(n, it=None):
                    dve.wait_ge(relu_ready, at(f0 + n + 1, it, 2))
                    a = n % 2
                    nc.vector.tensor_tensor(hid, ps[:, 1024 * a:1024 * a + 1024], relu_z,
                                            ALU.mult).then_inc(hid_ready, 1)

                def block(n, it=None, last=False):
                    u = u0 + 4 * n
                    if n:
                        for j in range(3):
                            lo(u + j + 2, it, 8)
                    if last:
                        jit(dn, 0)
                        square(n)
                        lo(u + 5)
                        jit(dn, 1)
                    else:
                        lo(u + 5, it, 8)
                        square(n, it)

                n = D_FF // 512
                block(0)
                block(1)
                with nc.vector.Fori(0, n // 2 - 2) as it:
                    block(2, it)
                    block(3, it)
                block(n - 2)
                block(n - 1, last=True)

            def attention(n, h0, latent):
                name, u_next = ("o", U_O) if latent else ("out", U_OUT)

                def copies(m, it=None):
                    dve.wait_ge(heads_turned, at(h0 + m + 1, it, 2))
                    if latent:
                        nc.vector.tensor_copy(qrT, ps[0:ROPE, 512:768]).then_inc(turned_dve, 1)
                    else:
                        nc.vector.tensor_copy(cuT[:, m % 2, 1:T + 1], ps[:, 512:768]).then_inc(turned_dve, 1)

                def conv(m, it=None):
                    y = feat[:, bass.ds(at((8 + m) * T, it, 2 * T), T)]
                    dve.wait_ge(turned_dve, at(m + 1, it, 2))

                    def tap(k):
                        g = G_ROW["taps"] + 8 * k + m
                        return gains[:, bass.ds(at(g, it, 2), 1)] if it is not None else gains[:, g:g + 1]
                    src = cuT[:, m % 2, :]
                    nc.vector.tensor_scalar(y, src[:, 1:T + 1], tap(1), None, ALU.mult).then_inc(taps, 1)
                    for i, k in ((1, 0), (2, 2)):
                        dve.wait_ge(taps, at(3 * m + i, it, 6))
                        nc.vector.scalar_tensor_tensor(y, src[:, k:T + k], tap(k), y, ALU.mult,
                                                       ALU.add).then_inc(taps, 1)

                def maxima(m, it=None):
                    dve.wait_ge(scores_ready, at(h0 + m + 1, it, 2))
                    b = 1024 + 512 * (m % 2)
                    nc.vector.tensor_reduce(nmax[:, m % 2, :],
                                            ps[:, b:b + 512].rearrange("p (q c) -> p q c", q=2),
                                            AX_X, ALU.max, negate=True).then_inc(max_ready, 1)

                def normalise(m, it=None):
                    dve.wait_ge(exp_ready, at(h0 + m + 1, it, 2))
                    nc.vector.reciprocal(rrec[:, m % 2, :], rsum[:, m % 2, :]).then_inc(recip_ready, 1)
                    dve.wait_ge(recip_ready, at(h0 + m + 1, it, 2))
                    for q in range(2):
                        pr = prob[m % 2][:, q * T:(q + 1) * T]
                        ins = nc.vector.tensor_scalar(pr, pr, rrec[:, m % 2, q:q + 1], None, ALU.mult)
                    ins.then_inc(probs_ready, 1)

                def take(m, it=None):
                    dve.wait_ge(heads_out, at(h0 + m + 1, it, 2))
                    nc.vector.tensor_copy(feat[:, bass.ds(at(m * T, it, 2 * T), T)],
                                          ps[:, 3072:3328]).then_inc(heads_ready, 1)

                for m, it in turns(nc.vector, n):
                    if 0 <= m < n:
                        maxima(m, it)
                    if 0 <= m + 1 < n:
                        copies(m + 1, it)
                    if 0 <= m < n and not latent:
                        conv(m, it)
                    if 0 <= m < n:
                        normalise(m, it)
                    if m == n - 2:
                        jit(name, 0)
                        jit(name, 1)
                    if m == n + 1:
                        lo(u_next + 1)
                    if 0 <= m - 2 < n:
                        take(m - 2, it)

            nc.vector.memset(cuT[:, :, :], 0.0).then_inc(consts_set, 1)
            dve.wait_ge(gains_ready, 1)
            turn_in("mix0")
            lo(U_IN + 5)
            with nc.vector.Fori(0, IN_A // 512 - 2) as it:
                for j in range(4):
                    lo(U_IN + j + 6, it, 4)
            for u in range(U_OUT - 2, U_OUT + 1):
                lo(u)
            dve.wait_ge(consts_set, 1)
            dve.wait_ge(kT_ready, 1)
            dve.sem_inc(heads_ready, HEADS_BASE)
            attention(HEADS_A, 0, False)
            dve.wait_ge(conv_ready, 8)
            dve.wait_ge(heads_ready, HEADS_BASE + HEADS_A)
            k_major("out")
            turn_in("mlp0")
            mlp_up(0)
            k_major("dn0")
            turn_in("mix1")
            for j in range(4):
                lo(U_CQ + j)

            def latent_low(i, name, k0):
                for k in range(4):
                    xs_low(k0 + k, X_BEFORE["lat"] + 4 * i + k + 1, 2048 + 1024 * i + k * T, G_ROW[name] + k)

            latent_low(0, "kv_lat", 0)
            lo(U_QKV)
            lo(U_QKV + 1, cols=8 * QH)
            latent_low(1, "q_lat", 4)
            pairs = HEADS_C // 2
            with nc.vector.Fori(0, pairs // 2 - 1) as it:
                for a in range(2):
                    lo_kv(U_QKV + 2 * a + 2, it, 4)
                    lo(U_QKV + 2 * a + 3, it, 4, cols=8 * QH)
            lo_kv(U_O - 2)
            lo(U_O - 1, cols=8 * QH)
            lo(U_O)
            attention(HEADS_C, HEADS_A, True)
            dve.wait_ge(heads_ready, HEADS_BASE + HEADS_A + HEADS_C)
            k_major("o")
            turn_in("mlp1")
            mlp_up(1)
            k_major("dn1")
            dve.wait_ge(rms2_ready, 2)
            for n in range(4):
                residual("final", n)
            dve.wait_ge(part_squares, 4 * TOK)
            nc.vector.tensor_reduce(sumsq[:, 4, :], sumsq_part[:, :, :], AX_X, ALU.add).then_inc(squares, TOK)
            dve.wait_ge(g_landed, 16)
            dve.wait_ge(rms_ready, 5)
            for i in range(4):
                t, c = i // 2, slice(D // 2 * (i % 2), D // 2 * (i % 2 + 1))
                nc.vector.scalar_tensor_tensor(final[:, t, c], h[:, t, c], rms[:, 4, t:t + 1], g_final[:, c],
                                               ALU.mult, ALU.mult).then_inc(final_ready, 1)

        @block.tensor
        def _(pe):
            def three(dst, x_hi, x_lo, wh, wl, first, last):
                nc.tensor.matmul(dst, x_hi, wh, start=first, stop=False)
                nc.tensor.matmul(dst, x_hi, wl, start=False, stop=False)
                return nc.tensor.matmul(dst, x_lo, wh, start=False, stop=last)

            def n_unit(u, ks, bank, first, last, it=None, per=0, cols=512, halfway=None):
                pe.wait_ge(lo_split, at(u + 1, it, per))
                s = u % SPLIT
                for i, k in enumerate(ks):
                    if i == 2 and halfway:
                        halfway()
                    c = slice(i * cols, (i + 1) * cols)
                    for t in range(TOK):
                        b = 512 * (bank + t)
                        tok = slice(t * P, (t + 1) * P)
                        ins = three(ps[:, b:b + cols], xs[:, k, 0, tok], xs[:, k, 1, tok],
                                    w_hi[:, s, c], w_lo[:, s, c],
                                    first and i == 0, last and i == len(ks) - 1)
                ins.then_inc(unit_used, 1)

            def n_block(u, bank, it=None, per=0, between=None):
                for j in range(4):
                    n_unit(u + j, range(4 * j, 4 * j + 4), bank, j == 0, j == 3, it, per)
                    if between:
                        between(j)

            def turn_stream(s, n):
                if s:
                    pe.wait_ge(h_ready, 4 * (s - 1) + n + 1)
                else:
                    pe.wait_ge(x_landed[n], 16)
                if s == 0 and n == 3:
                    pe.wait_ge(gains_ready, 1)
                for k in range(4):
                    for t in range(TOK):
                        c = 512 * n + 128 * k
                        b = 1024 * n + T * k + P * t
                        ins = nc.tensor.transpose(ps[:, b:b + P], h[:, t, c:c + P], ident[:, :])
                ins.then_inc(h_turned, 1)

            def k_major(name, order=range(4), before={}):
                u0, k0, n = K_PHASES[name]
                s_next = STAGES.index(NEXT[name])

                def unit(j, first, last, it=None):
                    u = u0 + j
                    pe.wait_ge(jit_lo, at(k0 + j + 1, it, 4))
                    pe.wait_ge(lo_split, at(u + 1, it, 4))
                    for i, c in enumerate(order if j == 0 else range(4)):
                        if j == 0 and c in before:
                            before[c]()
                        if last and c == 3 and s_next < 4:
                            turn_stream(s_next, 0)
                        for t in range(TOK):
                            b = 1024 * c + 512 * t
                            tok = slice(t * P, (t + 1) * P)
                            w = slice(512 * c, 512 * c + 512)
                            ins = three(ps[:, b:b + 512], js[:, j % SPLIT, 0, tok], js[:, j % SPLIT, 1, tok],
                                        w_hi[:, u % SPLIT, w], w_lo[:, u % SPLIT, w], first, last)
                        ins.then_inc(bank_pass if i < 3 else unit_used, 1)

                for j in range(4):
                    unit(j, j == 0, False)
                with nc.tensor.Fori(0, n // 4 - 2) as it:
                    for j in range(4):
                        unit(4 + j, False, False, it)
                for j in range(n - 4, n):
                    unit(j, False, j == n - 1)

            def turn_in(name):
                s, u0, x0 = STAGES.index(name), FIRST_UNIT[name], X_BEFORE[name]

                if s == 0:
                    turn_stream(s, 0)
                turn_stream(s, 1)
                for j in range(4):
                    pe.wait_ge(xs_lo, x0 + 4 * j + 4)
                    n_unit(u0 + j, range(4 * j, 4 * j + 4), 0, j == 0, j == 3)
                    if j < 2:
                        turn_stream(s, j + 2)

            def mlp_up(layer):
                u0, f0 = U_UP[layer], 16 * layer

                def turn(n, it=None):
                    pe.wait_ge(hid_ready, at(f0 + n + 1, it, 2))
                    for k in range(4):
                        for t in range(TOK):
                            b = 2048 + T * k + P * t
                            ins = nc.tensor.transpose(ps[:, b:b + P], hid[:, 512 * t + P * k:512 * t + P * k + P],
                                                      ident[:, :])
                    ins.then_inc(hid_turned, 1)

                def block(n, it=None):
                    n_block(u0 + 4 * n, 2 * (n % 2), it, 8, lambda j: turn(n - 1, it) if j == 2 else None)

                n = D_FF // 512
                block(1)
                with nc.tensor.Fori(0, n // 2 - 1) as it:
                    block(2, it)
                    block(3, it)
                k_major("dn%d" % layer, (0, 3, 1, 2),
                        {1: lambda: turn(n - 1), 2: lambda: pe.wait_ge(feat_ready, f0 + n)})

            def attention(n, h0, latent, ahead):
                def turn(m, it=None):
                    pe.wait_ge(staged, at(h0 + m + 1, it, 2))
                    if not latent:
                        pe.wait_ge(gate_staged, at(m + 1, it, 2))
                    if h0 + m:
                        pe.wait_ge(turned_act, at(h0 + m, it, 2))
                        pe.wait_ge(turned_dve, at(h0 + m, it, 2))
                    s = 768 * (m % 2)
                    for t in range(TOK):
                        if latent:
                            q = s + QH * t
                            nc.tensor.transpose(ps[:, P * t:P * t + P], stage[:, q:q + P], ident[:, :])
                            k = s + 2 * QH + P * t
                            nc.tensor.transpose(ps[:, T + P * t:T + P * t + P], stage[:, k:k + P], ident[:, :])
                            ins = nc.tensor.transpose(ps[0:ROPE, 512 + P * t:512 + P * t + P],
                                                      stage[:, q + P:q + QH], ident[:, :])
                        else:
                            for i, b in enumerate((0, 512, 2560)):
                                src = stage[:, s + T * i + P * t:s + T * i + P * t + P]
                                ins = nc.tensor.transpose(ps[:, b + P * t:b + P * t + P], src, ident[:, :])
                    ins.then_inc(heads_turned, 1)

                def scores(m, it=None):
                    pe.wait_ge(turned_act, at(h0 + m + 1, it, 2))
                    if latent:
                        pe.wait_ge(turned_dve, at(h0 + m + 1, it, 2))
                    if h0 + m >= 2:
                        pe.wait_ge(exp_ready, at(h0 + m - 1, it, 2))
                    for q in range(2):
                        b = 1024 + 512 * (m % 2) + T * q
                        tok = slice(P * q, P * q + P)
                        if latent:
                            nc.tensor.matmul(ps[:, b:b + T], qT[:, tok], knT, start=True, stop=False)
                            ins = nc.tensor.matmul(ps[:, b:b + T], qrT[:, tok], krT[:, :], start=False, stop=True)
                        else:
                            kv = m // 4
                            if it is not None:
                                keys = kT[:, bass.ds(at(0, it, T), T)]
                            else:
                                keys = kT[:, T * kv:T * kv + T]
                            ins = nc.tensor.matmul(ps[:, b:b + T], qT[:, tok], keys, start=True, stop=True)
                    ins.then_inc(scores_ready, 1)

                def turn_probs(m, it=None):
                    pe.wait_ge(probs_ready, at(h0 + m + 1, it, 2))
                    if h0 + m:
                        pe.wait_ge(probT_ready, at(h0 + m, it, 2))
                    for k in range(2):
                        for q in range(2):
                            b = 2048 + T * k + P * q
                            src = prob[m % 2][:, T * q + P * k:T * q + P * k + P]
                            ins = nc.tensor.transpose(ps[:, b:b + P], src, ident[:, :])
                    ins.then_inc(probs_turned, 1)

                def values(m, it=None):
                    pe.wait_ge(probT_ready, at(h0 + m + 1, it, 2))
                    pe.wait_ge(v_staged, at(h0 + m + 1, it, 2))
                    pe.wait_ge(heads_ready, at(HEADS_BASE + h0 + m, it, 2))
                    for k in range(2):
                        v = 1536 + T * (m % 2) + P * k
                        ins = nc.tensor.matmul(ps[:, 3072:3328], stage[:, v:v + P], probT[:, T * k:T * k + T],
                                               start=(k == 0), stop=(k == 1))
                    ins.then_inc(heads_out, 1)

                ahead(lambda: turn(0))
                for m, it in turns(nc.tensor, n):
                    if 0 <= m < n:
                        scores(m, it)
                    if 0 < m + 1 < n:
                        turn(m + 1, it)
                    if m == 1:
                        if latent:
                            pe.wait_ge(q_out, HEADS_C // 2)
                        else:
                            pe.wait_ge(mix_evac, IN_A // 512)
                    if 0 <= m - 2 < n - 2:
                        values(m - 2, it)
                    if 0 <= m - 1 < n - 1:
                        turn_probs(m - 1, it)

                def last_probs():
                    values(n - 2)
                    turn_probs(n - 1)
                    pe.wait_ge(exp_ready, h0 + n)
                k_major("o" if latent else "out", range(4), {
                    0: lambda: pe.wait_ge(turned_dve, h0 + n),
                    1: last_probs,
                    2: lambda: values(n - 1),
                    3: lambda: pe.wait_ge(heads_ready, HEADS_BASE + h0 + n)})

            pe.wait_ge(const_landed, 16 * 2)
            nc.tensor.transpose(ps[:, 3584:3584 + G_ROWS], gain_rows[:, :],
                                ident[0:G_ROWS, 0:G_ROWS]).then_inc(gains_turned, 1)
            turn_in("mix0")
            last = IN_A // 512 - 1
            with nc.tensor.Fori(0, last // 2 - 1) as it:
                for b in (1, 2):
                    n_block(U_IN + 4 * b, proj_bank(b), it, 8)
            n_block(U_IN + 4 * (last - 1), proj_bank(last - 1))

            def turn_keys():
                pe.wait_ge(qk_ready, 1)
                for g in range(KV_A):
                    for t in range(TOK):
                        b = 2048 + T * g + P * t
                        c = HEADS_A * HD + HD * g
                        ins = nc.tensor.transpose(ps[:, b:b + P], projA[:, t, c:c + HD], ident[:, :])
                ins.then_inc(k_turned, 1)

            def last_block(turn_first_head):
                n_block(U_IN + 4 * last, proj_bank(last),
                        between=lambda j: {1: turn_keys, 2: turn_first_head}.get(j, lambda: None)())
                pe.wait_ge(kT_ready, 1)

            attention(HEADS_A, 0, False, last_block)
            turn_in("mlp0")
            mlp_up(0)
            turn_in("mix1")
            pe.wait_ge(lo_split, U_KR + 1)
            s = U_KR % SPLIT
            for t in range(TOK):
                for k in range(KT):
                    tok, c, b = slice(t * P, (t + 1) * P), slice(ROPE * k, ROPE * k + ROPE), 512 * (6 + t)
                    ins = three(ps[:, b:b + ROPE], xs[:, k, 0, tok], xs[:, k, 1, tok],
                                w_hi[:, s, c], w_lo[:, s, c], k == 0, k == KT - 1)
            ins.then_inc(unit_used, 1)

            def turn_latent(which, bank):
                pe.wait_ge(lat_out, 2 - which)
                for k in range(4):
                    for t in range(TOK):
                        b = 512 * bank + T * k + P * t
                        ins = nc.tensor.transpose(ps[:, b:b + P], lat[:, which, t, P * k:P * k + P], ident[:, :])
                ins.then_inc(lat_turned, 1)

            def turn_key():
                pe.wait_ge(kr_roped, 1)
                pe.wait_ge(lat_sq, 2)
                for t in range(TOK):
                    ins = nc.tensor.transpose(ps[0:ROPE, P * t:P * t + P], kr[:, t, :], ident[:, :])
                ins.then_inc(kr_turned, 1)

            n_block(U_CQ, 2, between=lambda j: {1: lambda: turn_latent(1, 4), 2: turn_key}.get(j, lambda: None)())
            pe.wait_ge(xs_lo, X_BEFORE["lat"] + 4)
            pe.wait_ge(krT_ready, 1)

            def heads_pair(a, it=None, halfway=None):
                u, bank = U_QKV + 2 * a, 4 * (a % 2)
                n_unit(u, range(4), bank, True, True, it, 4, halfway=halfway)
                if halfway:
                    pe.wait_ge(xs_lo, X_BEFORE["lat"] + 8)
                n_unit(u + 1, range(4, 8), bank + 2, True, True, it, 4, cols=2 * QH)

            heads_pair(0, halfway=lambda: turn_latent(0, 6))
            heads_pair(1)
            with nc.tensor.Fori(0, HEADS_C // 4 - 1) as it:
                heads_pair(2, it)
                heads_pair(3, it)

            def first_head(turn_first_head):
                pe.wait_ge(q_out, HEADS_C // 2 - 1)
                turn_first_head()

            attention(HEADS_C, HEADS_A, True, first_head)
            turn_in("mlp1")
            mlp_up(1)

        @block.gpsimd
        def _(pool):
            steps = [0]

            def step(ins):
                steps[0] += 1
                ins.then_inc(pool_step, 1)
                pool.wait_ge(pool_step, steps[0])

            def waited(it):
                if it is not None:
                    pool.sem_inc(pool_waited, 1)

            def inverse_rms(s):
                pool.wait_ge(squares, TOK * (s + 1))
                step(nc.gpsimd.tensor_scalar(meansq[:, s, :], sumsq[:, s, :], 1.0 / D, NORM_EPS,
                                             ALU.mult, ALU.add))
                nc.gpsimd.tensor_tensor(rms[:, s, :], meansq[:, s, :], half[:, 0:TOK],
                                        ALU.pow).then_inc(rms_ready, 1)
                if s in (1, 3):
                    pool.wait_ge(rms_ready, s + 1)
                    nc.gpsimd.tensor_tensor(rms2[:, s // 2, :], rms[:, s, :], rms[:, s, :],
                                            ALU.mult).then_inc(rms2_ready, 1)

            def attention(n, h0, latent):
                def stage_head(m, it=None):
                    if h0 + m >= 2:
                        pool.wait_ge(heads_turned, at(h0 + m - 1, it, 2))
                        waited(it)
                    s = 768 * (m % 2)
                    if latent:
                        nc.gpsimd.tensor_copy(stage[:, s:s + 2 * QH].rearrange("p (t c) -> p t c", t=2),
                                              qC[:, :, bass.ds(at(QH * m, it, 2 * QH), QH)])
                        nc.gpsimd.tensor_copy(stage[:, s + 2 * QH:s + 2 * QH + T]
                                              .rearrange("p (t c) -> p t c", t=2),
                                              kvC[:, :, bass.ds(at(2 * HD * m, it, 4 * HD), HD)]
                                              ).then_inc(staged, 1)
                    else:
                        def to(i):
                            return stage[:, s + T * i:s + T * i + T].rearrange("p (t c) -> p t c", t=2)

                        def of(c):
                            return projA[:, :, bass.ds(at(c + HD * m, it, 2 * HD), HD)]
                        nc.gpsimd.tensor_copy(to(0), of(0))
                        nc.gpsimd.tensor_tensor(to(1), of(C_AT), of(U_AT), ALU.mult).then_inc(staged, 1)

                def stage_values(m, it=None):
                    if h0 + m >= 2:
                        pool.wait_ge(heads_out, at(h0 + m - 1, it, 2))
                        waited(it)
                    to = stage[:, 1536 + T * (m % 2):1536 + T * (m % 2) + T].rearrange("p (t c) -> p t c", t=2)
                    src = kvC[:, :, bass.ds(at(2 * HD * m + HD, it, 4 * HD), HD)]
                    nc.gpsimd.tensor_copy(to, src).then_inc(v_staged, 1)

                def gate(m, it=None):
                    y = feat[:, bass.ds(at((8 + m) * T, it, 2 * T), T)]
                    pool.wait_ge(taps, at(3 * m + 3, it, 6))
                    waited(it)
                    pool.wait_ge(turned_act, at(m + 1, it, 2))
                    waited(it)
                    nc.gpsimd.tensor_tensor(y, y, BT[m % 2], ALU.mult).then_inc(conv_ready, 1)

                stage_head(0)
                stage_head(1)
                if latent:
                    rope_queries(HEADS_C // 2 - 1)
                else:
                    pool.wait_ge(mix_evac, IN_A // 512)
                for m, it in turns(nc.gpsimd, n):
                    if m >= 0 and m + 2 < n:
                        stage_head(m + 2, it)
                    if 0 <= m < n:
                        if latent:
                            stage_values(m, it)
                        else:
                            gate(m, it)

            def rope_queries(i, it=None):
                tmp = [q_tmp[:, j, :].rearrange("p (t h c) -> p t h c", t=TOK, h=2) for j in range(4)]
                pool.wait_ge(q_out, at(i + 1, it, 1))
                waited(it)
                q = qC[:, :, bass.ds(at(2 * QH * i, it, 2 * QH), 2 * QH)].rearrange("p t (h c) -> p t h c", h=2)
                q = q[:, :, :, NOPE:QH].rearrange("p t h (c two) -> p t h c two", two=2)
                sh = [P, TOK, 2, ROPE // 2]
                cos, sin = (rope_c[:, s, :, :].unsqueeze(2).to_broadcast(sh) for s in range(2))
                for t, (part, f) in zip(tmp, ((0, cos), (1, sin), (0, sin), (1, cos))):
                    nc.gpsimd.tensor_tensor(t, q[:, :, :, :, part], f, ALU.mult).then_inc(q_prod, 1)
                pool.wait_ge(q_prod, at(4 * i + 4, it, 4))
                waited(it)
                nc.gpsimd.tensor_tensor(q[:, :, :, :, 0], tmp[0], tmp[1], ALU.subtract).then_inc(q_roped, 1)
                nc.gpsimd.tensor_tensor(q[:, :, :, :, 1], tmp[2], tmp[3], ALU.add).then_inc(q_roped, 1)
                pool.wait_ge(q_roped, at(2 * i + 2, it, 2))

            nc.gpsimd.memset(half[:, :], -0.5).then_inc(consts_set, 1)
            pool.wait_ge(consts_set, 2)
            inverse_rms(0)

            pool.wait_ge(mix_evac, 3)
            pool.wait_ge(rope_landed, 16 * 4)
            x = projA[:, :, 0:QK_A].rearrange("p t (h c) -> p t h c", c=HD)
            sq = tmpA.rearrange("p (t h c) -> p t h c", t=TOK, c=HD)
            step(nc.gpsimd.tensor_tensor(sq, x, x, ALU.mult))
            w = HD // 2
            while w >= 1:
                step(nc.gpsimd.tensor_tensor(sq[:, :, :, 0:w], sq[:, :, :, 0:w], sq[:, :, :, w:2 * w], ALU.add))
                w //= 2
            step(nc.gpsimd.tensor_scalar(head_ms[:, :].rearrange("p (t h) -> p t h", t=TOK),
                                         sq[:, :, :, 0:1].rearrange("p t h o -> p t (h o)"),
                                         1.0 / HD, NORM_EPS, ALU.mult, ALU.add))
            step(nc.gpsimd.tensor_tensor(head_r[:, :, :].rearrange("p t h -> p (t h)"), head_ms[:, :],
                                         half[:, 0:20], ALU.pow))
            step(nc.gpsimd.tensor_scalar(head_r[:, :, 0:HEADS_A], head_r[:, :, 0:HEADS_A],
                                         float(HD) ** -0.5, None, ALU.mult))
            n_heads = HEADS_A + KV_A
            step(nc.gpsimd.tensor_tensor(x, x, head_r[:, :, :].unsqueeze(3).to_broadcast([P, TOK, n_heads, HD]),
                                         ALU.mult))
            for g, (a, b) in enumerate(((0, HEADS_A), (HEADS_A, n_heads))):
                gain = gqk[:, HD * g:HD * g + HD].unsqueeze(1).unsqueeze(1).to_broadcast([P, TOK, b - a, HD])
                step(nc.gpsimd.tensor_tensor(x[:, :, a:b, :], x[:, :, a:b, :], gain, ALU.mult))
            pairs = projA[:, :, 0:QK_A].rearrange("p t (h c two) -> p t h c two", c=HD // 2, two=2)
            hc = [P, TOK, n_heads, HD // 2]
            half_n = TOK * n_heads * HD // 2
            prod = [tmpA[:, 0:half_n], tmpA[:, half_n:2 * half_n], stage[:, 0:half_n], work[:, 0:half_n]]
            prod = [a.rearrange("p (t h c) -> p t h c", t=TOK, h=n_heads) for a in prod]
            cos, sin = (ropeA[:, i].unsqueeze(2).to_broadcast(hc) for i in range(2))
            even, odd = pairs[:, :, :, :, 0], pairs[:, :, :, :, 1]
            step(nc.gpsimd.tensor_tensor(prod[0], even, cos, ALU.mult))
            step(nc.gpsimd.tensor_tensor(prod[1], odd, sin, ALU.mult))
            step(nc.gpsimd.tensor_tensor(prod[2], even, sin, ALU.mult))
            step(nc.gpsimd.tensor_tensor(prod[3], odd, cos, ALU.mult))
            step(nc.gpsimd.tensor_tensor(even, prod[0], prod[1], ALU.subtract))
            step(nc.gpsimd.tensor_tensor(odd, prod[2], prod[3], ALU.add))
            nc.gpsimd.memset(head_ms[:, 0:1], 0.0).then_inc(qk_ready, 1)
            pool.wait_ge(mix_evac, IN_A // 512 - 1)
            attention(HEADS_A, 0, False)
            inverse_rms(1)
            inverse_rms(2)

            pool.wait_ge(kr_out, 1)
            krp = kr.rearrange("p t (c two) -> p t c two", two=2)
            cos_c, sin_c = rope_c[:, 0, :, :], rope_c[:, 1, :, :]
            for i, (part, f) in enumerate(((0, cos_c), (1, sin_c), (0, sin_c), (1, cos_c))):
                step(nc.gpsimd.tensor_tensor(kr_tmp[:, i], krp[:, :, :, part], f, ALU.mult))
            step(nc.gpsimd.tensor_tensor(krp[:, :, :, 0], kr_tmp[:, 0], kr_tmp[:, 1], ALU.subtract))
            nc.gpsimd.tensor_tensor(krp[:, :, :, 1], kr_tmp[:, 2], kr_tmp[:, 3], ALU.add).then_inc(kr_roped, 1)

            pool.wait_ge(lat_sq, 4)
            r = rms[:, 2, :]
            for w in range(2):
                step(nc.gpsimd.tensor_tensor(lat_t[:, 0, w, :], lat_ss[:, w, :], r, ALU.mult))
                step(nc.gpsimd.tensor_tensor(lat_t[:, 1, w, :], lat_t[:, 0, w, :], r, ALU.mult))
                step(nc.gpsimd.tensor_scalar(lat_t[:, 2, w, :], lat_t[:, 1, w, :], 1.0 / LORA, NORM_EPS,
                                             ALU.mult, ALU.add))
                step(nc.gpsimd.tensor_tensor(lat_t[:, 0, w, :], lat_t[:, 2, w, :], half[:, 0:TOK], ALU.pow))
                if w == 0:
                    step(nc.gpsimd.tensor_scalar(lat_t[:, 0, w, :], lat_t[:, 0, w, :], float(QH) ** -0.5,
                                                 None, ALU.mult))
                ins = nc.gpsimd.tensor_tensor(lat_s[:, w, :], lat_t[:, 0, w, :], r, ALU.mult)
                if w == 0:
                    step(ins)
            ins.then_inc(lat_scale, 1)

            with nc.gpsimd.Fori(0, HEADS_C // 2 - 1) as it:
                rope_queries(0, it)
            pool.wait_ge(kv_out, HEADS_C // 2 - 1)
            attention(HEADS_C, HEADS_A, True)
            inverse_rms(3)
            inverse_rms(4)


def turns(engine, n):
    for m in (-1, 0, 1):
        yield m, None
    with engine.Fori(0, (n - 4) // 2) as it:
        for m in (2, 3):
            yield m, it
    for m in range(n - 2, n + 2):
        yield m, None


_INS = ["x", "even_w_in", "even_q_norm_g", "even_k_norm_g", "even_w_out", "odd_w_down", "odd_w_uq",
        "odd_w_ukv", "odd_w_o", "mlp_w_up", "mlp_w_down", "final_norm_g"]

_GAINS = [("even_norm_g", 0), ("mlp_norm_g", 0), ("odd_norm_g", 0), ("mlp_norm_g", 1),
          ("odd_q_lat_g", 0), ("odd_kv_lat_g", 0), ("even_conv_w", 0)]


def _rope_table(np, rot_dim, grid_w=64):
    t = np.arange(T)
    axis = rot_dim // 2
    exponent = -np.arange(0, axis, 2, dtype=np.float32) / np.float32(axis)
    inv = np.power(np.float32(10000.0), exponent, dtype=np.float32)
    row, col = (t // grid_w).astype(np.float32), (t % grid_w).astype(np.float32)
    ang = np.concatenate([row[:, None] * inv, col[:, None] * inv], axis=-1)
    both = np.stack([np.cos(ang), np.sin(ang)]).astype(np.float32)
    return np.ascontiguousarray(both.reshape(2, TOK, P, -1).transpose(2, 0, 1, 3))


def kernel(**inputs):
    import numpy as _np
    import concourse.bacc as _bacc
    from concourse import mybir as _mybir
    from concourse.bass_utils import run_bass_kernel_spmd as _run

    nc = _bacc.Bacc("TRN2", target_bir_lowering=False, num_devices=1, dynamic_dma_scratch_size=1024)
    arrays, args = {}, {}

    def give(name, a):
        a = _np.ascontiguousarray(a)
        arrays[f"in_{name}_dram"] = a
        args[name] = nc.dram_tensor(f"in_{name}_dram", a.shape, _mybir.dt.from_np(a.dtype),
                                    kind="ExternalInput").ap()

    for name in _INS:
        give(name, inputs[name])
    give("gain_rows", _np.concatenate([_np.asarray(inputs[name])[i].reshape(-1, P) for name, i in _GAINS]))
    give("ident", _np.eye(P, dtype=_np.float32))
    give("rope_a", _rope_table(_np, HD))
    give("rope_c", _rope_table(_np, ROPE))
    out = nc.dram_tensor("out_0_dram", (1, T, D), F32, kind="ExternalOutput").ap()
    build(nc, args, out)
    r = _run(nc, [arrays], core_ids=[0])
    return r.results[0]["out_0_dram"]
```

```python
from contextlib import ExitStack

import concourse.bass as bass
from concourse import mybir
from concourse.alu_op_type import AluOpType as ALU

ACT = mybir.ActivationFunctionType
F32 = mybir.dt.float32
F32R = mybir.dt.float32r
BF16 = mybir.dt.bfloat16
AX_X = mybir.AxisListType.X

P = 128
D = 2048
TOK = 2
T = TOK * P
KT = D // P
NORM_EPS = 1e-6

HEADS_A, KV_A, HD = 8, 2, 128
QK_A = (HEADS_A + KV_A) * HD
IN_A = 4608
B_AT, C_AT, U_AT = 1536, 2560, 3584
HEADS_C, NOPE, ROPE = 16, 128, 64
QH = NOPE + ROPE
LORA = 512
D_FF = 8192

UNIT = 2048
RAW = 4
SPLIT = 2

U_IN = 0
U_OUT = U_IN + 4 * (IN_A // 512)
U_UP = [0, 0]
U_DN = [0, 0]
U_UP[0] = U_OUT + KT
U_DN[0] = U_UP[0] + 4 * (D_FF // 512)
U_CKV = U_DN[0] + D_FF // P
U_KR = U_CKV + 4
U_CQ = U_KR + 1
U_QKV = U_CQ + 4
U_O = U_QKV + HEADS_C
U_UP[1] = U_O + KT
U_DN[1] = U_UP[1] + 4 * (D_FF // 512)
U_END = U_DN[1] + D_FF // P

K_OUT, K_DN0, K_O, K_DN1 = 0, KT, KT + D_FF // P, 2 * KT + D_FF // P

X_BEFORE = {"mix0": 0, "mlp0": 16, "mix1": 32, "lat": 48, "mlp1": 56}
STAGES = ["mix0", "mlp0", "mix1", "mlp1", "final"]

G_ROW = {"mix0": 0, "mlp0": 16, "mix1": 32, "mlp1": 48, "q_lat": 64, "kv_lat": 68, "taps": 72}
G_ROWS = 96


HEADS_BASE = 1


def at(c, it=None, per=0):
    return c if it is None else it * per + c


def landed_count(u, it=None, per=0):
    return at(16 * (u // RAW + 1), it, 16 * per // RAW)


def build(nc, A, out):
    ctx = ExitStack()
    with ctx:
        def sb(name, shape, dt=F32):
            return ctx.enter_context(nc.sbuf_tensor(name, shape, dt))

        def sem(name):
            return ctx.enter_context(nc.semaphore(name))

        ps = ctx.enter_context(nc.psum_tensor("ps", [P, 8 * 512], F32))
        h = sb("h", [P, TOK, D])
        xs = sb("xs", [P, KT, 2, T], F32R)
        raw = sb("raw", [P, RAW, UNIT])
        w_hi = sb("w_hi", [P, SPLIT, UNIT], F32R)
        w_lo = sb("w_lo", [P, SPLIT, UNIT], F32R)
        js = sb("js", [P, SPLIT, 2, T], F32R)
        big = sb("big", [P, 18432])
        work = sb("work", [P, 3072])
        stage = sb("stage", [P, 2048])
        ident = sb("ident", [P, P])
        gain_rows = sb("gain_rows", [G_ROWS, P])
        gains = sb("gains", [P, G_ROWS])
        rope_c = sb("rope_c", [P, 2, TOK, ROPE // 2])
        krT = sb("krT", [ROPE, T])
        sumsq = sb("sumsq", [P, 5, TOK])
        sumsq_part = sb("sumsq_part", [P, TOK, 4])
        meansq = sb("meansq", [P, 5, TOK])
        rms = sb("rms", [P, 5, TOK])
        rms2 = sb("rms2", [P, 2, TOK])
        half = sb("half", [P, 24])
        lat_ss = sb("lat_ss", [P, 2, TOK])
        lat_t = sb("lat_t", [P, 3, 2, TOK])
        lat_s = sb("lat_s", [P, 2, TOK])
        head_ms = sb("head_ms", [P, 2 * 10])
        head_r = sb("head_r", [P, 2, 10])
        nmax = sb("nmax", [P, 2, 2])
        rsum = sb("rsum", [P, 2, 2])
        rrec = sb("rrec", [P, 2, 2])

        feat = big[:, 0:64 * T]
        projA = big[:, 4096:4096 + 2 * IN_A].rearrange("p (t c) -> p t c", t=TOK)
        tmpA = big[:, 13312:13312 + 2 * QK_A]
        kT = big[:, 15872:15872 + KV_A * T]
        ropeA = big[:, 16384:16640].rearrange("p (s t c) -> p s t c", s=2, t=TOK)
        gqk = big[:, 16640:16896]
        lat = big[:, 0:2048].rearrange("p (w t c) -> p w t c", w=2, t=TOK)
        kr = big[:, 2048:2176].rearrange("p (t c) -> p t c", t=TOK)
        kr_tmp = big[:, 2176:2432].rearrange("p (j t c) -> p j t c", j=4, t=TOK)
        q_tmp = big[:, 2432:2944].rearrange("p (j c) -> p j c", j=4)
        qC = big[:, 4096:4096 + 2 * 3072].rearrange("p (t c) -> p t c", t=TOK)
        kvC = big[:, 10240:10240 + 2 * 4096].rearrange("p (t c) -> p t c", t=TOK)
        g_final = big[:, 16384:18432]
        final = big[:, 0:2 * D].rearrange("p (t c) -> p t c", t=TOK)

        hid, side_z = work[:, 0:1024], work[:, 1024:2048]
        qT, knT, qrT = work[:, 0:256], work[:, 256:512], work[0:ROPE, 2560:2816]
        prob = [work[:, 512 + 512 * i:1024 + 512 * i] for i in range(2)]
        probT = work[:, 1536:2048]
        BT = [work[:, 2048 + 256 * i:2304 + 256 * i] for i in range(2)]
        cuT = sb("cuT", [P, 2, T + 2])

        raw_landed = [sem(f"raw_landed{i}") for i in range(RAW)]
        const_landed, g_landed = sem("const_landed"), sem("g_landed")
        hi_split, lo_split, unit_used = sem("hi_split"), sem("lo_split"), sem("unit_used")
        jit_hi, jit_lo = sem("jit_hi"), sem("jit_lo")
        bank_pass = sem("bank_pass")
        gains_turned, gains_ready = sem("gains_turned"), sem("gains_ready")
        consts_set = sem("consts_set")
        h_ready, h_turned = sem("h_ready"), sem("h_turned")
        xs_hi, xs_lo = sem("xs_hi"), sem("xs_lo")
        half_landed = sem("half_landed")
        half_split = sem("half_split")
        squares, part_squares, rms_ready = sem("squares"), sem("part_squares"), sem("rms_ready")
        rms2_ready = sem("rms2_ready")
        mix_evac = sem("mix_evac")
        pool_step = sem("pool_step")
        qk_ready = sem("qk_ready")
        k_turned, kT_ready = sem("k_turned"), sem("kT_ready")
        staged, gate_staged, v_staged = sem("staged"), sem("gate_staged"), sem("v_staged")
        heads_turned, turned_act, turned_dve = sem("heads_turned"), sem("turned_act"), sem("turned_dve")
        scores_ready, max_ready, exp_ready = sem("scores_ready"), sem("max_ready"), sem("exp_ready")
        recip_ready, probs_ready = sem("recip_ready"), sem("probs_ready")
        probs_turned, probT_ready = sem("probs_turned"), sem("probT_ready")
        heads_out, heads_ready = sem("heads_out"), sem("heads_ready")
        taps, conv_ready = sem("taps"), sem("conv_ready")
        side_ready, hid_ready, feat_ready = sem("side_ready"), sem("hid_ready"), sem("feat_ready")
        kr_flat, kr_back = sem("kr_flat"), sem("kr_back")
        kr_out, kr_roped, kr_turned, krT_ready = sem("kr_out"), sem("kr_roped"), sem("kr_turned"), sem("krT_ready")
        lat_out, lat_sq, lat_turned, lat_scale = sem("lat_out"), sem("lat_sq"), sem("lat_turned"), sem("lat_scale")
        kv_out, q_out, q_prod, q_roped = sem("kv_out"), sem("q_out"), sem("q_prod"), sem("q_roped")
        pool_waited, act_waited = sem("pool_waited"), sem("act_waited")
        last_pass, last_h = sem("last_pass"), sem("last_h")
        gained, scaled_act, scaled_dve, stored = (sem("gained"), sem("scaled_act"), sem("scaled_dve"),
                                                  sem("stored"))
        x_landed = [sem(f"x_landed{n}") for n in range(4)]
        rope_landed = sem("rope_landed")

        block = ctx.enter_context(nc.Block())

        K_PHASES = {"out": (U_OUT, K_OUT, KT), "dn0": (U_DN[0], K_DN0, D_FF // P),
                    "o": (U_O, K_O, KT), "dn1": (U_DN[1], K_DN1, D_FF // P)}
        AFTER = {"mlp0": "out", "mix1": "dn0", "mlp1": "o", "final": "dn1"}
        NEXT = {product: stage for stage, product in AFTER.items()}

        def proj_bank(b):
            return 2 if b % 2 else 6

        def turned_at(name, k):
            return (k - 12 if name == "mix0" and k >= 12 else k) * T

        FIRST_UNIT = {"mix0": U_IN, "mlp0": U_UP[0], "mix1": U_CKV, "mlp1": U_UP[1]}

        @block.sync
        def _(sp):
            def load(u, src, cols, it=None, per=0):
                if u >= RAW:
                    sp.wait_ge(lo_split, at(u - RAW + 1, it, per))
                s = u % RAW
                dst = raw[:, s, 0:cols]
                if len(src.shape) == 3:
                    dst = dst.rearrange("p (k c) -> p k c", k=src.shape[1])
                sp.dma_start(dst, src).then_inc(raw_landed[s], 16)

            def tiles(w):
                return w.rearrange("(k p) c -> p k c", p=P)

            w = tiles(A["even_w_in"][0])
            x = A["x"][0].rearrange("(t p) c -> p t c", p=P)

            def load_x(n):
                sp.dma_start(h[:, :, 512 * n:512 * n + 512], x[:, :, 512 * n:512 * n + 512]
                             ).then_inc(x_landed[n], 16)

            load_x(0)
            sp.dma_start(gain_rows[:, :], A["gain_rows"]).then_inc(const_landed, 16)
            for i, landed in enumerate((half_landed, raw_landed[0])):
                sp.dma_start(raw[:, 0, UNIT // 2 * i:UNIT // 2 * (i + 1)].rearrange("p (k c) -> p k c", k=2),
                             w[:, 2 * i:2 * i + 2, 0:512]).then_inc(landed, 16)
            for j in range(1, RAW):
                load_x(j)
                load(U_IN + j, w[:, 4 * j:4 * j + 4, 0:512], UNIT)
            sp.dma_start(ropeA, A["rope_a"]).then_inc(rope_landed, 16)
            sp.dma_start(rope_c[:, :, :, :], A["rope_c"]).then_inc(rope_landed, 16)
            sp.dma_start(gqk[:, 0:HD], A["even_q_norm_g"].to_broadcast([P, HD])).then_inc(rope_landed, 16)
            sp.dma_start(gqk[:, HD:2 * HD], A["even_k_norm_g"].to_broadcast([P, HD])).then_inc(rope_landed, 16)
            with nc.sync.Fori(0, IN_A // 512 - 1) as it:
                for j in range(4):
                    load(U_IN + 4 + j, w[:, 4 * j:4 * j + 4, bass.ds(at(512, it, 512), 512)], UNIT, it, 4)

            def k_major(w, u0, n):
                w = w.rearrange("(g k p) c -> p g k c", p=P, k=4)
                with nc.sync.Fori(0, n // 4) as it:
                    for j in range(4):
                        load(u0 + j, w[:, bass.ds(it, 1), j, :].rearrange("p g c -> p (g c)"), UNIT, it, 4)

            def n_major(w, u0, blocks):
                w = tiles(w)
                with nc.sync.Fori(0, blocks) as it:
                    for j in range(4):
                        load(u0 + j, w[:, 4 * j:4 * j + 4, bass.ds(at(0, it, 512), 512)], UNIT, it, 4)

            k_major(A["even_w_out"][0], U_OUT, KT)
            n_major(A["mlp_w_up"][0], U_UP[0], D_FF // 512)
            k_major(A["mlp_w_down"][0], U_DN[0], D_FF // P)
            w = tiles(A["odd_w_down"][0])
            for j in range(4):
                load(U_CKV + j, w[:, 4 * j:4 * j + 4, LORA:2 * LORA], UNIT)
            load(U_KR, w[:, :, 2 * LORA:2 * LORA + ROPE], KT * ROPE)
            for j in range(4):
                load(U_CQ + j, w[:, 4 * j:4 * j + 4, 0:LORA], UNIT)
            wq, wkv = tiles(A["odd_w_uq"][0]), tiles(A["odd_w_ukv"][0])
            with nc.sync.Fori(0, HEADS_C // 4) as it:
                for a in range(2):
                    load(U_QKV + 2 * a, wkv[:, :, bass.ds(at(512 * a, it, 1024), 512)], UNIT, it, 4)
                    load(U_QKV + 2 * a + 1, wq[:, :, bass.ds(at(2 * QH * a, it, 4 * QH), 2 * QH)],
                         8 * QH, it, 4)
            k_major(A["odd_w_o"][0], U_O, KT)
            sp.wait_ge(heads_ready, HEADS_BASE + HEADS_A + HEADS_C)
            sp.dma_start(g_final, A["final_norm_g"].rearrange("(a c) -> a c", a=1)
                         .to_broadcast([P, D])).then_inc(g_landed, 16)
            n_major(A["mlp_w_up"][1], U_UP[1], D_FF // 512)
            k_major(A["mlp_w_down"][1], U_DN[1], D_FF // P)
            for t, c, n, done, count in ((0, 0, 2, scaled_act, 1), (0, 2, 2, scaled_dve, 1),
                                         (1, 2, 1, scaled_dve, 2), (1, 0, 2, scaled_act, 2),
                                         (1, 3, 1, scaled_dve, 3)):
                c = slice(512 * c, 512 * (c + n))
                sp.wait_ge(done, count)
                sp.dma_start(out[0, t * P:(t + 1) * P, c], final[:, t, c]).then_inc(stored, 16)
            sp.wait_ge(stored, 16 * 5)

        @block.scalar
        def _(act):
            act.dma_start(ident[:, :], A["ident"]).then_inc(const_landed, 16)

            def hi(u, it=None, per=0, cols=UNIT):
                act.wait_ge(raw_landed[u % RAW], landed_count(u, it, per))
                if u >= SPLIT:
                    act.wait_ge(unit_used, at(u - SPLIT + 1, it, per))
                nc.scalar.activation(w_hi[:, u % SPLIT, 0:cols], raw[:, u % RAW, 0:cols],
                                     ACT.Copy).then_inc(hi_split, 1)

            def hi_halves(u, it=None, per=0):
                if u >= SPLIT:
                    act.wait_ge(unit_used, at(u - SPLIT + 1, it, per))
                for i, done in enumerate((half_split, hi_split)):
                    if u == U_IN and i == 0:
                        act.wait_ge(half_landed, 16)
                    else:
                        act.wait_ge(raw_landed[u % RAW], landed_count(u, it, per))
                    c = slice(UNIT // 2 * i, UNIT // 2 * (i + 1))
                    nc.scalar.activation(w_hi[:, u % SPLIT, c], raw[:, u % RAW, c], ACT.Copy).then_inc(done, 1)

            def turn_in(name):
                s, u0 = STAGES.index(name), FIRST_UNIT[name]

                def high(n):
                    act.wait_ge(h_turned, 4 * s + n + 1)
                    for k in range(4 * n, 4 * n + 4):
                        b = turned_at(name, k)
                        nc.scalar.activation(xs[:, k, 0, :], ps[:, b:b + T], ACT.Copy,
                                             scale=gains[:, G_ROW[name] + k:G_ROW[name] + k + 1]
                                             ).then_inc(xs_hi, 1)

                if name == "mix0":
                    hi_halves(u0)
                high(0)
                high(1)
                hi(u0 + 1)
                high(2)
                hi(u0 + 2)
                square(s, 0)
                hi(u0 + 3)
                high(3)
                square(s, 1)
                hi(u0 + 4, cols=KT * ROPE if u0 + 4 == U_KR else UNIT)
                act.wait_ge(squares, TOK * s + TOK)

            def waited(it):
                if it is not None:
                    act.sem_inc(act_waited, 1)

            def square(s, t):
                if s:
                    act.wait_ge(h_ready, 4 * s)
                else:
                    for n in range(4):
                        act.wait_ge(x_landed[n], 16)
                if s or t:
                    act.wait_ge(squares, TOK * s + t)
                nc.scalar.activation(work[:, 0:D], h[:, t, :], ACT.Square,
                                     accum_out=sumsq[:, s, t:t + 1]).then_inc(squares, 1)

            def jit(name, k, it=None):
                u0, k0, n = K_PHASES[name]
                if k >= SPLIT:
                    act.wait_ge(unit_used, at(u0 + k - SPLIT + 1, it, 4))
                nc.scalar.activation(js[:, k % SPLIT, 0, :], feat[:, bass.ds(at(k * T, it, 4 * T), T)],
                                     ACT.Copy).then_inc(jit_hi, 1)

            def k_major(name, skip_next=False):
                u0, k0, n = K_PHASES[name]
                with nc.scalar.Fori(0, n // 4 - 1) as it:
                    for j in range(4):
                        jit(name, j + 2, it)
                        hi(u0 + j + 2, it, 4)
                for j in range(n - 4, n):
                    if j + 2 < n:
                        jit(name, j + 2)
                        hi(u0 + j + 2)
                    elif j + 2 == n and not skip_next:
                        hi(u0 + n)

            def attention(n, h0, latent, ahead, last_out):
                name, u_next = ("o", U_O) if latent else ("out", U_OUT)

                def copies(m, it=None):
                    act.wait_ge(heads_turned, at(h0 + m + 1, it, 2))
                    if latent:
                        nc.scalar.activation(work[:, 0:512], ps[:, 0:512], ACT.Copy).then_inc(turned_act, 1)
                    else:
                        nc.scalar.activation(qT, ps[:, 0:256], ACT.Copy)
                        if m >= 2:
                            act.wait_ge(conv_ready, at(m - 1, it, 2))
                        nc.scalar.activation(BT[m % 2], ps[:, 2560:2816], ACT.Copy).then_inc(turned_act, 1)

                def stage_gate(m, it=None):
                    if m >= 2:
                        act.wait_ge(heads_turned, at(m - 1, it, 2))
                        waited(it)
                    s = 768 * (m % 2) + 2 * T
                    nc.scalar.activation(stage[:, s:s + T].rearrange("p (t c) -> p t c", t=2),
                                         projA[:, :, bass.ds(at(B_AT + HD * m, it, 2 * HD), HD)],
                                         ACT.Copy).then_inc(gate_staged, 1)

                def stage_values(m, it=None):
                    if m >= 2:
                        act.wait_ge(heads_out, at(m - 1, it, 2))
                        waited(it)
                    s = 1536 + T * (m % 2)
                    if it is not None:
                        src = projA[:, :, bass.ds(at(QK_A, it, HD), HD)]
                    else:
                        src = projA[:, :, QK_A + HD * (m // 4):QK_A + HD * (m // 4) + HD]
                    nc.scalar.activation(stage[:, s:s + T].rearrange("p (t c) -> p t c", t=2), src,
                                         ACT.Copy).then_inc(v_staged, 1)

                def exps(m, it=None):
                    act.wait_ge(max_ready, at(h0 + m + 1, it, 2))
                    if h0 + m >= 2:
                        act.wait_ge(probs_turned, at(h0 + m - 1, it, 2))
                    b = 1024 + 512 * (m % 2)
                    for q in range(2):
                        ins = nc.scalar.activation(prob[m % 2][:, q * T:(q + 1) * T],
                                                   ps[:, b + q * T:b + (q + 1) * T], ACT.Exp,
                                                   bias=nmax[:, m % 2, q:q + 1],
                                                   accum_out=rsum[:, m % 2, q:q + 1])
                    ins.then_inc(exp_ready, 1)

                def turned(m, it=None):
                    act.wait_ge(probs_turned, at(h0 + m + 1, it, 2))
                    nc.scalar.activation(probT, ps[:, 2048:2560], ACT.Copy).then_inc(probT_ready, 1)

                if not latent:
                    act.wait_ge(qk_ready, 1)
                    stage_gate(0)
                ahead()
                for m, it in turns(nc.scalar, n):
                    if 0 <= m + 1 < n:
                        copies(m + 1, it)
                    if not latent and m + 2 < n:
                        stage_gate(m + 2, it)
                    if 0 <= m < n:
                        exps(m, it)
                        if not latent:
                            stage_values(m, it)
                    if m == -1:
                        last_out()
                    if m == n - 2:
                        act.wait_ge(heads_ready, HEADS_BASE + h0 + 2)
                        jit(name, 0)
                        jit(name, 1)
                    if 0 <= m - 1 < n:
                        turned(m - 1, it)
                hi(u_next + 1)

            def mlp_up(layer):
                u0, dn, n = U_UP[layer], "dn%d" % layer, D_FF // 512

                def side(i, it=None):
                    act.wait_ge(unit_used, at(u0 + 4 * i + 4, it, 8))
                    if (n - 1) * layer + i > 1:
                        act.wait_ge(hid_ready, at(n * layer + i, it, 2))
                    b = 2048 * (i % 2)
                    z = ps[:, b:b + 2048].rearrange("p (m s t) -> p m s t", m=4, s=2)
                    nc.scalar.activation(side_z.rearrange("p (m t) -> p m t", m=4), z[:, :, 1, :],
                                         ACT.Copy).then_inc(side_ready, 1)

                def block(i, it=None, last=False):
                    u = u0 + 4 * i
                    for j in range(3):
                        hi(u + j + 2, it, 8)
                    if last:
                        act.wait_ge(feat_ready, n * layer + 1)
                        jit(dn, 0)
                        jit(dn, 1)
                        side(i)
                        hi(u + 5)
                    else:
                        hi(u + 5, it, 8)
                        side(i, it)

                hi(u0 + 5)
                block(1)
                with nc.scalar.Fori(0, n // 2 - 2) as it:
                    block(2, it)
                    block(3, it)
                block(n - 2)
                block(n - 1, last=True)

            act.wait_ge(gains_turned, 1)
            nc.scalar.activation(gains[:, :], ps[:, 3584:3584 + G_ROWS], ACT.Copy).then_inc(gains_ready, 1)
            act.wait_ge(gains_ready, 1)
            turn_in("mix0")
            act.wait_ge(rms_ready, 1)

            def project(b, it=None):
                act.wait_ge(unit_used, at(U_IN + 4 * b + 4, it, 8))
                for t in range(TOK):
                    z = 512 * (proj_bank(b) + t)
                    ins = nc.scalar.activation(projA[:, t, bass.ds(at(512 * b, it, 1024), 512)],
                                               ps[:, z:z + 512], ACT.Copy, scale=rms[:, 0, t:t + 1])
                ins.then_inc(mix_evac, 1)

            hi(U_IN + 5)
            project(0)
            last = IN_A // 512 - 1
            with nc.scalar.Fori(0, last // 2 - 1) as it:
                for b in (1, 2):
                    for j in range(4):
                        hi(U_IN + 4 * b + j + 2, it, 8)
                    project(b, it)
            for j in range(4):
                hi(U_IN + 4 * last + j - 2)
            project(last - 1)

            def last_block():
                hi(U_IN + 4 * last + 2)
                hi(U_IN + 4 * last + 3)
                act.wait_ge(k_turned, 1)
                nc.scalar.activation(kT, ps[:, 2048:2560], ACT.Copy).then_inc(kT_ready, 1)
                hi(U_OUT)

            attention(HEADS_A, 0, False, last_block, lambda: project(last))

            act.wait_ge(heads_ready, HEADS_BASE + HEADS_A)
            act.wait_ge(conv_ready, HEADS_A)
            k_major("out")
            turn_in("mlp0")
            mlp_up(0)
            act.wait_ge(feat_ready, D_FF // 512)
            k_major("dn0")
            turn_in("mix1")

            def latent_out(which, bank):
                nc.scalar.activation(lat[:, which, :, :].rearrange("p t c -> p (t c)"),
                                     ps[:, 512 * bank:512 * bank + 1024], ACT.Copy).then_inc(lat_out, 1)
                for t in range(TOK):
                    if which == 0 or t:
                        act.wait_ge(lat_sq, (2 if which == 0 else 0) + t)
                    nc.scalar.activation(work[:, 0:512], ps[:, 512 * (bank + t):512 * (bank + t) + 512],
                                         ACT.Square, accum_out=lat_ss[:, which, t:t + 1]).then_inc(lat_sq, 1)

            hi(U_CQ)
            act.wait_ge(unit_used, U_CKV + 4)
            latent_out(1, 0)
            act.wait_ge(unit_used, U_KR + 1)
            nc.scalar.activation(krT[:, :], ps[0:ROPE, 3072:3072 + T], ACT.Copy).then_inc(kr_flat, 1)
            hi(U_CQ + 1)
            hi(U_CQ + 2)
            act.wait_ge(kr_back, 1)
            act.wait_ge(rms_ready, 3)
            for t in range(TOK):
                ins = nc.scalar.activation(kr[:, t, :], ps[:, 3584 + ROPE * t:3584 + ROPE * t + ROPE],
                                           ACT.Copy, scale=rms[:, 2, t:t + 1])
            ins.then_inc(kr_out, 1)
            hi(U_CQ + 3)

            def latent_high(which, name, k0):
                act.wait_ge(lat_turned, 2 - which)
                for k in range(4):
                    b = 2048 + 1024 * (1 - which) + k * T
                    nc.scalar.activation(xs[:, k0 + k, 0, :], ps[:, b:b + T], ACT.Copy,
                                         scale=gains[:, G_ROW[name] + k:G_ROW[name] + k + 1]
                                         ).then_inc(xs_hi, 1)

            latent_high(1, "kv_lat", 0)
            hi(U_QKV)
            act.wait_ge(kr_turned, 1)
            nc.scalar.activation(krT[:, :], ps[0:ROPE, 0:T], ACT.Copy).then_inc(krT_ready, 1)
            act.wait_ge(unit_used, U_CQ + 4)
            latent_out(0, 2)
            hi(U_QKV + 1, cols=8 * QH)
            latent_high(0, "q_lat", 4)
            act.wait_ge(lat_scale, 1)

            def pair_out(a, q, it=None):
                act.wait_ge(unit_used, at(U_QKV + 2 * a + q + 1, it, 4))
                for t in range(TOK):
                    b = 2048 * (a % 2) + 1024 * q + 512 * t
                    if q:
                        dst = qC[:, t, bass.ds(at(2 * QH * a, it, 4 * QH), 2 * QH)]
                        ins = nc.scalar.activation(dst, ps[:, b:b + 2 * QH], ACT.Copy,
                                                   scale=lat_s[:, 0, t:t + 1])
                    else:
                        dst = kvC[:, t, bass.ds(at(512 * a, it, 1024), 512)]
                        ins = nc.scalar.activation(dst, ps[:, b:b + 512], ACT.Copy,
                                                   scale=lat_s[:, 1, t:t + 1])
                ins.then_inc(q_out if q else kv_out, 1)

            pairs = HEADS_C // 2
            with nc.scalar.Fori(0, pairs // 2 - 1) as it:
                for a in range(2):
                    hi_halves(U_QKV + 2 * a + 2, it, 4)
                    pair_out(a, 0, it)
                    hi(U_QKV + 2 * a + 3, it, 4, cols=8 * QH)
                    pair_out(a, 1, it)
            hi_halves(U_O - 2)
            pair_out(pairs - 2, 0)
            hi(U_O - 1, cols=8 * QH)
            pair_out(pairs - 2, 1)

            def last_keys():
                hi(U_O)
                pair_out(pairs - 1, 0)

            attention(HEADS_C, HEADS_A, True, last_keys, lambda: pair_out(pairs - 1, 1))
            act.wait_ge(heads_ready, HEADS_BASE + HEADS_A + HEADS_C)
            k_major("o")
            turn_in("mlp1")
            mlp_up(1)
            act.wait_ge(feat_ready, 2 * D_FF // 512)
            k_major("dn1", skip_next=True)
            def last_square(t, n):
                i = 4 * t + n
                act.wait_ge(last_h, i + 1)
                nc.scalar.activation(work[:, 256 * i:256 * i + 256].bitcast(BF16), h[:, t, 512 * n:512 * n + 512],
                                     ACT.Square, accum_out=sumsq_part[:, t, n:n + 1]).then_inc(part_squares, 1)

            def scale(t):
                act.wait_ge(rms_ready, 5 + t)
                act.wait_ge(gained, 2 + 2 * t)
                nc.scalar.activation(final[:, t, 0:1024], final[:, t, 0:1024], ACT.Copy,
                                     scale=rms[:, 4, t:t + 1]).then_inc(scaled_act, 1)

            for t, n in ((0, 0), (0, 1), (0, 2), (0, 3), (1, 0), (1, 1)):
                last_square(t, n)
            scale(0)
            last_square(1, 2)
            last_square(1, 3)
            scale(1)

        @block.vector
        def _(dve):
            def lo(u, it=None, per=0, cols=UNIT):
                dve.wait_ge(hi_split, at(u + 1, it, per))
                nc.vector.tensor_tensor(w_lo[:, u % SPLIT, 0:cols], raw[:, u % RAW, 0:cols],
                                        w_hi[:, u % SPLIT, 0:cols].bitcast(F32),
                                        ALU.subtract).then_inc(lo_split, 1)

            def lo_halves(u, halves, it=None, per=0):
                for i in range(2):
                    if i == 0:
                        dve.wait_ge(half_split, at(halves, it, per // 2))
                    else:
                        dve.wait_ge(hi_split, at(u + 1, it, per))
                    c = slice(UNIT // 2 * i, UNIT // 2 * (i + 1))
                    ins = nc.vector.tensor_tensor(w_lo[:, u % SPLIT, c], raw[:, u % RAW, c],
                                                  w_hi[:, u % SPLIT, c].bitcast(F32), ALU.subtract)
                ins.then_inc(lo_split, 1)

            def xs_low(k, x_count, b, g):
                dve.wait_ge(xs_hi, x_count + (k + 1) % 2)
                nc.vector.scalar_tensor_tensor(xs[:, k, 1, :], ps[:, b:b + T], gains[:, g:g + 1],
                                               xs[:, k, 0, :].bitcast(F32), ALU.mult,
                                               ALU.subtract).then_inc(xs_lo, 1)

            def residual(name, n):
                s = STAGES.index(name)
                u0, k0, count = K_PHASES[AFTER[name]]
                if n < 3:
                    dve.wait_ge(bank_pass, 3 * (k0 + count - 1) + n + 1)
                else:
                    dve.wait_ge(unit_used, u0 + count)
                for t in range(TOK):
                    b, to = 1024 * n + 512 * t, h[:, t, 512 * n:512 * n + 512]
                    if name == "mix1":
                        ins = nc.vector.scalar_tensor_tensor(to, ps[:, b:b + 512],
                                                             rms2[:, 0, t:t + 1], to,
                                                             ALU.mult, ALU.add)
                    else:
                        ins = nc.vector.tensor_tensor(to, ps[:, b:b + 512], to, ALU.add)
                ins.then_inc(h_ready, 1)

            def turn_in(name):
                u0, first = FIRST_UNIT[name], name == "mix0"

                def low(n):
                    for k in range(4 * n, 4 * n + 4):
                        xs_low(k, X_BEFORE[name] + k + 1, turned_at(name, k), G_ROW[name] + k)
                if name == "mix1":
                    dve.wait_ge(rms2_ready, 1)
                if not first:
                    residual(name, 0)
                    residual(name, 1)
                if first:
                    lo_halves(u0, 1)
                else:
                    lo(u0)
                low(0)
                if not first:
                    residual(name, 2)
                low(1)
                lo(u0 + 1)
                if not first:
                    residual(name, 3)
                low(2)
                lo(u0 + 2)
                lo(u0 + 3)
                low(3)
                lo(u0 + 4, cols=KT * ROPE if u0 + 4 == U_KR else UNIT)

            def jit(name, k, it=None):
                dve.wait_ge(jit_hi, at(K_PHASES[name][1] + k + 1, it, 4))
                nc.vector.tensor_tensor(js[:, k % SPLIT, 1, :], feat[:, bass.ds(at(k * T, it, 4 * T), T)],
                                        js[:, k % SPLIT, 0, :].bitcast(F32),
                                        ALU.subtract).then_inc(jit_lo, 1)

            def k_major(name):
                u0, k0, n = K_PHASES[name]
                with nc.vector.Fori(0, n // 4 - 1) as it:
                    for j in range(4):
                        jit(name, j + 2, it)
                        lo(u0 + j + 2, it, 4)
                for j in range(n - 4, n):
                    if j + 2 < n:
                        jit(name, j + 2)
                        lo(u0 + j + 2)

            def mlp_up(layer):
                blocks = D_FF // 512
                u0, f0, dn = U_UP[layer], blocks * layer, "dn%d" % layer

                def activate(n, it=None):
                    dve.wait_ge(unit_used, at(u0 + 4 * n + 4, it, 8))
                    if n == 0:
                        dve.wait_ge(squares, TOK * (STAGES.index("mlp%d" % layer) + 1))
                        nc.vector.tensor_copy(hid, ps[:, 0:4 * T]).then_inc(hid_ready, 1)
                    else:
                        dve.wait_ge(feat_ready, at(f0 + n, it, 2))
                        b = 2048 * (n % 2)
                        z = ps[:, b:b + 2048].rearrange("p (m s t) -> p m s t", m=4, s=2)
                        dve.wait_ge(side_ready, at((blocks - 1) * layer + n, it, 2))
                        nc.vector.tensor_tensor(hid.rearrange("p (m t) -> p m t", m=4), z[:, :, 0, :],
                                                side_z.rearrange("p (m t) -> p m t", m=4),
                                                ALU.add).then_inc(hid_ready, 1)
                    dve.wait_ge(hid_ready, at(f0 + n + 1, it, 2))
                    nc.vector.scalar_tensor_tensor(feat[:, bass.ds(at(n * 4 * T, it, 8 * T), 4 * T)], hid,
                                                   0.0, hid, ALU.max, ALU.mult).then_inc(feat_ready, 1)

                def block(n, it=None, last=False):
                    u = u0 + 4 * n
                    if n:
                        for j in range(3):
                            lo(u + j + 2, it, 8)
                    if last:
                        jit(dn, 0)
                        jit(dn, 1)
                        activate(n)
                        lo(u + 5)
                    else:
                        lo(u + 5, it, 8)
                        activate(n, it)

                n = D_FF // 512
                block(0)
                block(1)
                with nc.vector.Fori(0, n // 2 - 2) as it:
                    block(2, it)
                    block(3, it)
                block(n - 2)
                block(n - 1, last=True)

            def attention(n, h0, latent):
                name, u_next = ("o", U_O) if latent else ("out", U_OUT)

                def copies(m, it=None):
                    dve.wait_ge(heads_turned, at(h0 + m + 1, it, 2))
                    if latent:
                        nc.vector.tensor_copy(qrT, ps[0:ROPE, 512:768]).then_inc(turned_dve, 1)
                    else:
                        if m >= 2:
                            dve.wait_ge(taps, at(3 * m - 3, it, 6))
                        nc.vector.tensor_copy(cuT[:, m % 2, 1:T + 1], ps[:, 512:768]).then_inc(turned_dve, 1)

                def tap(m, k, it=None):
                    y = feat[:, bass.ds(at((8 + m) * T, it, 2 * T), T)]
                    g = G_ROW["taps"] + 8 * k + m
                    gain = gains[:, bass.ds(at(g, it, 2), 1)] if it is not None else gains[:, g:g + 1]
                    src = cuT[:, m % 2, k:T + k]
                    if k == 1:
                        dve.wait_ge(turned_dve, at(m + 1, it, 2))
                        nc.vector.tensor_scalar(y, src, gain, None, ALU.mult).then_inc(taps, 1)
                    else:
                        dve.wait_ge(taps, at(3 * m + 1 + k // 2, it, 6))
                        nc.vector.scalar_tensor_tensor(y, src, gain, y, ALU.mult, ALU.add).then_inc(taps, 1)

                def maxima(m, it=None):
                    dve.wait_ge(scores_ready, at(h0 + m + 1, it, 2))
                    b = 1024 + 512 * (m % 2)
                    nc.vector.tensor_reduce(nmax[:, m % 2, :],
                                            ps[:, b:b + 512].rearrange("p (q c) -> p q c", q=2),
                                            AX_X, ALU.max, negate=True).then_inc(max_ready, 1)

                def normalise(m, it=None):
                    dve.wait_ge(exp_ready, at(h0 + m + 1, it, 2))
                    nc.vector.reciprocal(rrec[:, m % 2, :], rsum[:, m % 2, :]).then_inc(recip_ready, 1)
                    if not latent:
                        tap(m, 2, it)
                    dve.wait_ge(recip_ready, at(h0 + m + 1, it, 2))
                    for q in range(2):
                        pr = prob[m % 2][:, q * T:(q + 1) * T]
                        ins = nc.vector.tensor_scalar(pr, pr, rrec[:, m % 2, q:q + 1], None, ALU.mult)
                    ins.then_inc(probs_ready, 1)

                def take(m, it=None):
                    dve.wait_ge(heads_out, at(h0 + m + 1, it, 2))
                    nc.vector.tensor_copy(feat[:, bass.ds(at(m * T, it, 2 * T), T)],
                                          ps[:, 3072:3328]).then_inc(heads_ready, 1)

                for m, it in turns(nc.vector, n):
                    if 0 <= m < n:
                        maxima(m, it)
                        if not latent:
                            tap(m, 1, it)
                    if 0 <= m + 1 < n:
                        copies(m + 1, it)
                    if 0 <= m < n:
                        if not latent:
                            tap(m, 0, it)
                        normalise(m, it)
                    if m == n - 2:
                        jit(name, 0)
                        jit(name, 1)
                    if 0 <= m - 2 < n:
                        take(m - 2, it)
                lo(u_next + 1)

            nc.vector.memset(cuT[:, :, :], 0.0).then_inc(consts_set, 1)
            dve.wait_ge(gains_ready, 1)
            turn_in("mix0")
            lo(U_IN + 5)
            with nc.vector.Fori(0, IN_A // 512 - 2) as it:
                for j in range(4):
                    lo(U_IN + j + 6, it, 4)
            for u in range(U_OUT - 2, U_OUT + 1):
                lo(u)
            dve.wait_ge(consts_set, 1)
            dve.wait_ge(kT_ready, 1)
            dve.sem_inc(heads_ready, HEADS_BASE)
            attention(HEADS_A, 0, False)
            dve.wait_ge(conv_ready, 8)
            dve.wait_ge(heads_ready, HEADS_BASE + HEADS_A)
            k_major("out")
            turn_in("mlp0")
            mlp_up(0)
            k_major("dn0")
            turn_in("mix1")
            for j in range(4):
                lo(U_CQ + j)

            def latent_low(i, name, k0):
                for k in range(4):
                    xs_low(k0 + k, X_BEFORE["lat"] + 4 * i + k + 1, 2048 + 1024 * i + k * T, G_ROW[name] + k)

            latent_low(0, "kv_lat", 0)
            lo(U_QKV)
            lo(U_QKV + 1, cols=8 * QH)
            latent_low(1, "q_lat", 4)
            pairs = HEADS_C // 2
            with nc.vector.Fori(0, pairs // 2 - 1) as it:
                for a in range(2):
                    lo_halves(U_QKV + 2 * a + 2, a + 2, it, 4)
                    lo(U_QKV + 2 * a + 3, it, 4, cols=8 * QH)
            lo_halves(U_O - 2, 1 + pairs - 1)
            lo(U_O - 1, cols=8 * QH)
            lo(U_O)
            attention(HEADS_C, HEADS_A, True)
            dve.wait_ge(heads_ready, HEADS_BASE + HEADS_A + HEADS_C)
            k_major("o")
            turn_in("mlp1")
            mlp_up(1)
            k_major("dn1")
            dve.wait_ge(rms2_ready, 2)
            def last_sum(t, n):
                b, to = 1024 * n + 512 * t, h[:, t, 512 * n:512 * n + 512]
                dve.wait_ge(last_pass, 4 * t + n + 1)
                nc.vector.scalar_tensor_tensor(to, ps[:, b:b + 512], rms2[:, 1, t:t + 1], to,
                                               ALU.mult, ALU.add).then_inc(last_h, 1)

            def last_sumsq(t):
                dve.wait_ge(part_squares, 4 * t + 4)
                nc.vector.tensor_reduce(sumsq[:, 4, t:t + 1], sumsq_part[:, t, :], AX_X,
                                        ALU.add).then_inc(squares, 1)

            def scale(t, n, blocks):
                c = slice(512 * n, 512 * (n + blocks))
                dve.wait_ge(rms_ready, 5 + t)
                nc.vector.scalar_tensor_tensor(final[:, t, c], h[:, t, c], rms[:, 4, t:t + 1], g_final[:, c],
                                               ALU.mult, ALU.mult).then_inc(scaled_dve, 1)

            for n in range(4):
                last_sum(0, n)
            last_sum(1, 0)
            last_sumsq(0)
            for n in range(1, 4):
                last_sum(1, n)
            dve.wait_ge(g_landed, 16)
            scale(0, 2, 2)
            last_sumsq(1)
            scale(1, 2, 1)
            scale(1, 3, 1)

        @block.tensor
        def _(pe):
            def three(dst, stands_hi, stands_lo, moves_hi, moves_lo, first, last):
                nc.tensor.matmul(dst, stands_hi, moves_hi, start=first, stop=False)
                nc.tensor.matmul(dst, stands_hi, moves_lo, start=False, stop=False)
                return nc.tensor.matmul(dst, stands_lo, moves_hi, start=False, stop=last)

            def n_unit(u, ks, bank, first, last, it=None, per=0, cols=512, halfway=None,
                       split_by=None):
                pe.wait_ge(lo_split, at(u + 1, it, per))
                s = u % SPLIT
                for i, k in enumerate(ks):
                    if i == 2 and halfway:
                        halfway()
                    if split_by is not None:
                        pe.wait_ge(xs_lo, split_by + k + 1)
                    c = slice(i * cols, (i + 1) * cols)
                    for t in range(TOK):
                        b = 512 * (bank + t)
                        tok = slice(t * P, (t + 1) * P)
                        ins = three(ps[:, b:b + cols], xs[:, k, 0, tok], xs[:, k, 1, tok],
                                    w_hi[:, s, c], w_lo[:, s, c],
                                    first and i == 0, last and i == len(ks) - 1)
                ins.then_inc(unit_used, 1)

            def n_block(u, bank, it=None, per=0, between=None):
                for j in range(4):
                    n_unit(u + j, range(4 * j, 4 * j + 4), bank, j == 0, j == 3, it, per)
                    if between:
                        between(j)

            def turn_stream(s, n):
                if s:
                    pe.wait_ge(h_ready, 4 * (s - 1) + n + 1)
                else:
                    pe.wait_ge(x_landed[n], 16)
                for k in range(4):
                    for t in range(TOK):
                        c = 512 * n + 128 * k
                        b = turned_at(STAGES[s], 4 * n + k) + P * t
                        ins = nc.tensor.transpose(ps[:, b:b + P], h[:, t, c:c + P], ident[:, :])
                ins.then_inc(h_turned, 1)

            def k_major(name, before={}):
                u0, k0, n = K_PHASES[name]
                s_next = STAGES.index(NEXT[name])

                def unit(j, first, last, it=None):
                    u = u0 + j
                    pe.wait_ge(jit_lo, at(k0 + j + 1, it, 4))
                    pe.wait_ge(lo_split, at(u + 1, it, 4))
                    for c in range(4):
                        if j == 0 and c in before:
                            before[c]()
                        if last and c == 3 and s_next < 4:
                            turn_stream(s_next, 0)
                        for t in range(TOK):
                            b = 1024 * c + 512 * t
                            tok = slice(t * P, (t + 1) * P)
                            w = slice(512 * c, 512 * c + 512)
                            ins = three(ps[:, b:b + 512], js[:, j % SPLIT, 0, tok], js[:, j % SPLIT, 1, tok],
                                        w_hi[:, u % SPLIT, w], w_lo[:, u % SPLIT, w], first, last)
                        ins.then_inc(bank_pass if c < 3 else unit_used, 1)

                for j in range(4):
                    unit(j, j == 0, False)
                with nc.tensor.Fori(0, n // 4 - 2) as it:
                    for j in range(4):
                        unit(4 + j, False, False, it)
                if name != "dn1":
                    for j in range(n - 4, n):
                        unit(j, False, j == n - 1)
                    return
                for j in range(n - 4, n - 1):
                    unit(j, False, False)
                j, u = n - 1, u0 + n - 1
                pe.wait_ge(jit_lo, k0 + j + 1)
                pe.wait_ge(lo_split, u + 1)
                for t in range(TOK):
                    for c in range(4):
                        b, w = 1024 * c + 512 * t, slice(512 * c, 512 * c + 512)
                        tok = slice(t * P, (t + 1) * P)
                        three(ps[:, b:b + 512], js[:, j % SPLIT, 0, tok], js[:, j % SPLIT, 1, tok],
                              w_hi[:, u % SPLIT, w], w_lo[:, u % SPLIT, w], False, True).then_inc(last_pass, 1)

            def turn_in(name):
                s, u0, x0 = STAGES.index(name), FIRST_UNIT[name], X_BEFORE[name]

                if s == 0:
                    turn_stream(s, 0)
                turn_stream(s, 1)
                for j in range(4):
                    if s:
                        pe.wait_ge(xs_lo, x0 + 4 * j + 4)
                        if name == "mix1":
                            n_unit(u0 + j, range(4 * j, 4 * j + 4), 0, j == 0, j == 3)
                        else:
                            up_first(u0 + j, j)
                    else:
                        if j == 0:
                            pe.wait_ge(gains_ready, 1)
                        n_unit(u0 + j, range(4 * j, 4 * j + 4), proj_bank(0), j == 0, j == 3, split_by=x0)
                    if j < 2:
                        turn_stream(s, j + 2)

            def up_first(u, j):
                pe.wait_ge(lo_split, u + 1)
                s = u % SPLIT
                for m in range(4):
                    for i in range(4):
                        k, w = 4 * j + i, slice(512 * i + P * m, 512 * i + P * m + P)
                        ins = three(ps[:, T * m:T * m + T], w_hi[:, s, w], w_lo[:, s, w], xs[:, k, 0, :],
                                    xs[:, k, 1, :], k == 0 and m % 2 == 0, k == KT - 1 and m % 2 == 1)
                ins.then_inc(unit_used, 1)

            def mlp_up(layer):
                u0, f0, n = U_UP[layer], D_FF // 512 * layer, D_FF // 512

                def unit(u, j, bank, it):
                    pe.wait_ge(lo_split, at(u + 1, it, 8))
                    s = u % SPLIT
                    for m in range(4):
                        b = 512 * (bank + m)
                        for i in range(4):
                            k, w = 4 * j + i, slice(512 * i + P * m, 512 * i + P * m + P)

                            def high(first, last):
                                return nc.tensor.matmul(ps[:, b:b + 512], w_hi[:, s, w],
                                                        xs[:, k, :, :].rearrange("p s t -> p (s t)"),
                                                        start=first, stop=last)

                            def low():
                                return nc.tensor.matmul(ps[:, b:b + T], w_lo[:, s, w], xs[:, k, 0, :],
                                                        start=False, stop=False)
                            if k < KT - 1:
                                high(k == 0, False)
                                ins = low()
                            else:
                                low()
                                ins = high(False, True)
                    return ins

                def block(n, it=None):
                    if n > 1:
                        pe.wait_ge(hid_ready, at(f0 + n - 1, it, 2))
                    for j in range(4):
                        unit(u0 + 4 * n + j, j, 4 * (n % 2), it).then_inc(unit_used, 1)

                block(1)
                with nc.tensor.Fori(0, n // 2 - 1) as it:
                    block(2, it)
                    block(3, it)
                k_major("dn%d" % layer, before={0: lambda: pe.wait_ge(hid_ready, f0 + n - 1),
                                                2: lambda: pe.wait_ge(hid_ready, f0 + n)})

            def attention(n, h0, latent, ahead):
                def turn(m, it=None):
                    pe.wait_ge(staged, at(h0 + m + 1, it, 2))
                    if not latent:
                        pe.wait_ge(gate_staged, at(m + 1, it, 2))
                    if h0 + m:
                        pe.wait_ge(turned_act, at(h0 + m, it, 2))
                        pe.wait_ge(turned_dve, at(h0 + m, it, 2))
                    s = 768 * (m % 2)
                    for t in range(TOK):
                        if latent:
                            q = s + QH * t
                            nc.tensor.transpose(ps[:, P * t:P * t + P], stage[:, q:q + P], ident[:, :])
                            k = s + 2 * QH + P * t
                            nc.tensor.transpose(ps[:, T + P * t:T + P * t + P], stage[:, k:k + P], ident[:, :])
                            ins = nc.tensor.transpose(ps[0:ROPE, 512 + P * t:512 + P * t + P],
                                                      stage[:, q + P:q + QH], ident[:, :])
                        else:
                            for i, b in enumerate((0, 512, 2560)):
                                src = stage[:, s + T * i + P * t:s + T * i + P * t + P]
                                ins = nc.tensor.transpose(ps[:, b + P * t:b + P * t + P], src, ident[:, :])
                    ins.then_inc(heads_turned, 1)

                def scores(m, it=None):
                    pe.wait_ge(turned_act, at(h0 + m + 1, it, 2))
                    if latent:
                        pe.wait_ge(turned_dve, at(h0 + m + 1, it, 2))
                    if h0 + m >= 2:
                        pe.wait_ge(exp_ready, at(h0 + m - 1, it, 2))
                    for q in range(2):
                        b = 1024 + 512 * (m % 2) + T * q
                        tok = slice(P * q, P * q + P)
                        if latent:
                            nc.tensor.matmul(ps[:, b:b + T], qT[:, tok], knT, start=True, stop=False)
                            ins = nc.tensor.matmul(ps[:, b:b + T], qrT[:, tok], krT[:, :], start=False, stop=True)
                        else:
                            kv = m // 4
                            if it is not None:
                                keys = kT[:, bass.ds(at(0, it, T), T)]
                            else:
                                keys = kT[:, T * kv:T * kv + T]
                            ins = nc.tensor.matmul(ps[:, b:b + T], qT[:, tok], keys, start=True, stop=True)
                    ins.then_inc(scores_ready, 1)

                def turn_probs(m, it=None):
                    pe.wait_ge(probs_ready, at(h0 + m + 1, it, 2))
                    if h0 + m:
                        pe.wait_ge(probT_ready, at(h0 + m, it, 2))
                    for k in range(2):
                        for q in range(2):
                            b = 2048 + T * k + P * q
                            src = prob[m % 2][:, T * q + P * k:T * q + P * k + P]
                            ins = nc.tensor.transpose(ps[:, b:b + P], src, ident[:, :])
                    ins.then_inc(probs_turned, 1)

                def values(m, it=None):
                    pe.wait_ge(probT_ready, at(h0 + m + 1, it, 2))
                    pe.wait_ge(v_staged, at(h0 + m + 1, it, 2))
                    pe.wait_ge(heads_ready, at(HEADS_BASE + h0 + m, it, 2))
                    for k in range(2):
                        v = 1536 + T * (m % 2) + P * k
                        ins = nc.tensor.matmul(ps[:, 3072:3328], stage[:, v:v + P], probT[:, T * k:T * k + T],
                                               start=(k == 0), stop=(k == 1))
                    ins.then_inc(heads_out, 1)

                ahead(lambda: turn(0))
                for m, it in turns(nc.tensor, n):
                    if 0 <= m < n:
                        scores(m, it)
                    if 0 < m + 1 < n:
                        turn(m + 1, it)
                    if m == 1:
                        if latent:
                            pe.wait_ge(q_out, HEADS_C // 2)
                        else:
                            pe.wait_ge(mix_evac, IN_A // 512)
                    if 0 <= m - 2 < n - 2:
                        values(m - 2, it)
                    if 0 <= m - 1 < n - 1:
                        turn_probs(m - 1, it)

                def last_probs():
                    values(n - 2)
                    turn_probs(n - 1)
                    pe.wait_ge(exp_ready, h0 + n)
                k_major("o" if latent else "out", {
                    0: lambda: pe.wait_ge(turned_dve, h0 + n),
                    1: last_probs,
                    2: lambda: values(n - 1),
                    3: lambda: pe.wait_ge(heads_ready, HEADS_BASE + h0 + n)})

            pe.wait_ge(const_landed, 16 * 2)
            nc.tensor.transpose(ps[:, 3584:3584 + G_ROWS], gain_rows[:, :],
                                ident[0:G_ROWS, 0:G_ROWS]).then_inc(gains_turned, 1)
            turn_in("mix0")
            last = IN_A // 512 - 1
            with nc.tensor.Fori(0, last // 2 - 1) as it:
                for b in (1, 2):
                    n_block(U_IN + 4 * b, proj_bank(b), it, 8)
            n_block(U_IN + 4 * (last - 1), proj_bank(last - 1))

            def turn_keys():
                pe.wait_ge(qk_ready, 1)
                for g in range(KV_A):
                    for t in range(TOK):
                        b = 2048 + T * g + P * t
                        c = HEADS_A * HD + HD * g
                        ins = nc.tensor.transpose(ps[:, b:b + P], projA[:, t, c:c + HD], ident[:, :])
                ins.then_inc(k_turned, 1)

            def last_block(turn_first_head):
                n_block(U_IN + 4 * last, proj_bank(last),
                        between=lambda j: {1: turn_keys, 2: turn_first_head}.get(j, lambda: None)())
                pe.wait_ge(kT_ready, 1)

            attention(HEADS_A, 0, False, last_block)
            turn_in("mlp0")
            mlp_up(0)
            turn_in("mix1")
            pe.wait_ge(lo_split, U_KR + 1)
            s = U_KR % SPLIT
            for k in range(KT):
                c = slice(ROPE * k, ROPE * k + ROPE)
                ins = three(ps[0:ROPE, 3072:3072 + T], w_hi[:, s, c], w_lo[:, s, c],
                            xs[:, k, 0, :], xs[:, k, 1, :], k == 0, k == KT - 1)
            ins.then_inc(unit_used, 1)

            def turn_key_back():
                pe.wait_ge(kr_flat, 1)
                for t in range(TOK):
                    ins = nc.tensor.transpose(ps[:, 3584 + ROPE * t:3584 + ROPE * t + ROPE],
                                              krT[:, P * t:P * t + P], ident[0:ROPE, 0:ROPE])
                ins.then_inc(kr_back, 1)

            def turn_latent(which, bank):
                pe.wait_ge(lat_out, 2 - which)
                for k in range(4):
                    for t in range(TOK):
                        b = 512 * bank + T * k + P * t
                        ins = nc.tensor.transpose(ps[:, b:b + P], lat[:, which, t, P * k:P * k + P], ident[:, :])
                ins.then_inc(lat_turned, 1)

            def turn_key():
                pe.wait_ge(kr_roped, 1)
                pe.wait_ge(lat_sq, 2)
                for t in range(TOK):
                    ins = nc.tensor.transpose(ps[0:ROPE, P * t:P * t + P], kr[:, t, :], ident[:, :])
                ins.then_inc(kr_turned, 1)

            n_block(U_CQ, 2, between=lambda j: {0: turn_key_back, 1: lambda: turn_latent(1, 4),
                                                2: turn_key}.get(j, lambda: None)())
            pe.wait_ge(xs_lo, X_BEFORE["lat"] + 4)
            pe.wait_ge(krT_ready, 1)

            def heads_pair(a, it=None, halfway=None):
                u, bank = U_QKV + 2 * a, 4 * (a % 2)
                n_unit(u, range(4), bank, True, True, it, 4, halfway=halfway)
                if halfway:
                    pe.wait_ge(xs_lo, X_BEFORE["lat"] + 8)
                n_unit(u + 1, range(4, 8), bank + 2, True, True, it, 4, cols=2 * QH)

            heads_pair(0, halfway=lambda: turn_latent(0, 6))
            heads_pair(1)
            with nc.tensor.Fori(0, HEADS_C // 4 - 1) as it:
                heads_pair(2, it)
                heads_pair(3, it)

            def first_head(turn_first_head):
                pe.wait_ge(q_out, HEADS_C // 2 - 1)
                turn_first_head()

            attention(HEADS_C, HEADS_A, True, first_head)
            turn_in("mlp1")
            mlp_up(1)

        @block.gpsimd
        def _(pool):
            steps = [0]

            def step(ins):
                steps[0] += 1
                ins.then_inc(pool_step, 1)
                pool.wait_ge(pool_step, steps[0])

            def waited(it):
                if it is not None:
                    pool.sem_inc(pool_waited, 1)

            def inverse_rms(s):
                pool.wait_ge(squares, TOK * (s + 1))
                step(nc.gpsimd.tensor_scalar(meansq[:, s, :], sumsq[:, s, :], 1.0 / D, NORM_EPS,
                                             ALU.mult, ALU.add))
                nc.gpsimd.tensor_tensor(rms[:, s, :], meansq[:, s, :], half[:, 0:TOK],
                                        ALU.pow).then_inc(rms_ready, 1)
                if s in (1, 3):
                    pool.wait_ge(rms_ready, s + 1)
                    nc.gpsimd.tensor_tensor(rms2[:, s // 2, :], rms[:, s, :], rms[:, s, :],
                                            ALU.mult).then_inc(rms2_ready, 1)

            def attention(n, h0, latent):
                def stage_head(m, it=None):
                    if h0 + m >= 2:
                        pool.wait_ge(heads_turned, at(h0 + m - 1, it, 2))
                        waited(it)
                    s = 768 * (m % 2)
                    if latent:
                        nc.gpsimd.tensor_copy(stage[:, s:s + 2 * QH].rearrange("p (t c) -> p t c", t=2),
                                              qC[:, :, bass.ds(at(QH * m, it, 2 * QH), QH)])
                        nc.gpsimd.tensor_copy(stage[:, s + 2 * QH:s + 2 * QH + T]
                                              .rearrange("p (t c) -> p t c", t=2),
                                              kvC[:, :, bass.ds(at(2 * HD * m, it, 4 * HD), HD)]
                                              ).then_inc(staged, 1)
                    else:
                        def to(i):
                            return stage[:, s + T * i:s + T * i + T].rearrange("p (t c) -> p t c", t=2)

                        def of(c):
                            return projA[:, :, bass.ds(at(c + HD * m, it, 2 * HD), HD)]
                        nc.gpsimd.tensor_copy(to(0), of(0))
                        nc.gpsimd.tensor_tensor(to(1), of(C_AT), of(U_AT), ALU.mult).then_inc(staged, 1)

                def stage_values(m, it=None):
                    if h0 + m >= 2:
                        pool.wait_ge(heads_out, at(h0 + m - 1, it, 2))
                        waited(it)
                    to = stage[:, 1536 + T * (m % 2):1536 + T * (m % 2) + T].rearrange("p (t c) -> p t c", t=2)
                    src = kvC[:, :, bass.ds(at(2 * HD * m + HD, it, 4 * HD), HD)]
                    nc.gpsimd.tensor_copy(to, src).then_inc(v_staged, 1)

                def gate(m, it=None):
                    y = feat[:, bass.ds(at((8 + m) * T, it, 2 * T), T)]
                    pool.wait_ge(taps, at(3 * m + 3, it, 6))
                    waited(it)
                    pool.wait_ge(turned_act, at(m + 1, it, 2))
                    waited(it)
                    nc.gpsimd.tensor_tensor(y, y, BT[m % 2], ALU.mult).then_inc(conv_ready, 1)

                stage_head(0)
                stage_head(1)
                if latent:
                    rope_queries(HEADS_C // 2 - 1)
                else:
                    pool.wait_ge(mix_evac, IN_A // 512)
                for m, it in turns(nc.gpsimd, n):
                    if m >= 0 and m + 2 < n:
                        stage_head(m + 2, it)
                    if 0 <= m < n:
                        if latent:
                            stage_values(m, it)
                        else:
                            gate(m, it)

            def rope_queries(i, it=None):
                tmp = [q_tmp[:, j, :].rearrange("p (t h c) -> p t h c", t=TOK, h=2) for j in range(4)]
                pool.wait_ge(q_out, at(i + 1, it, 1))
                waited(it)
                q = qC[:, :, bass.ds(at(2 * QH * i, it, 2 * QH), 2 * QH)].rearrange("p t (h c) -> p t h c", h=2)
                q = q[:, :, :, NOPE:QH].rearrange("p t h (c two) -> p t h c two", two=2)
                sh = [P, TOK, 2, ROPE // 2]
                cos, sin = (rope_c[:, s, :, :].unsqueeze(2).to_broadcast(sh) for s in range(2))
                for t, (part, f) in zip(tmp, ((0, cos), (1, sin), (0, sin), (1, cos))):
                    nc.gpsimd.tensor_tensor(t, q[:, :, :, :, part], f, ALU.mult).then_inc(q_prod, 1)
                pool.wait_ge(q_prod, at(4 * i + 4, it, 4))
                waited(it)
                nc.gpsimd.tensor_tensor(q[:, :, :, :, 0], tmp[0], tmp[1], ALU.subtract).then_inc(q_roped, 1)
                nc.gpsimd.tensor_tensor(q[:, :, :, :, 1], tmp[2], tmp[3], ALU.add).then_inc(q_roped, 1)
                pool.wait_ge(q_roped, at(2 * i + 2, it, 2))

            nc.gpsimd.memset(half[:, :], -0.5).then_inc(consts_set, 1)
            pool.wait_ge(consts_set, 2)
            inverse_rms(0)

            pool.wait_ge(mix_evac, 3)
            pool.wait_ge(rope_landed, 16 * 4)
            x = projA[:, :, 0:QK_A].rearrange("p t (h c) -> p t h c", c=HD)
            sq = tmpA.rearrange("p (t h c) -> p t h c", t=TOK, c=HD)
            step(nc.gpsimd.tensor_tensor(sq, x, x, ALU.mult))
            w = HD // 2
            while w >= 1:
                step(nc.gpsimd.tensor_tensor(sq[:, :, :, 0:w], sq[:, :, :, 0:w], sq[:, :, :, w:2 * w], ALU.add))
                w //= 2
            step(nc.gpsimd.tensor_scalar(head_ms[:, :].rearrange("p (t h) -> p t h", t=TOK),
                                         sq[:, :, :, 0:1].rearrange("p t h o -> p t (h o)"),
                                         1.0 / HD, NORM_EPS, ALU.mult, ALU.add))
            step(nc.gpsimd.tensor_tensor(head_r[:, :, :].rearrange("p t h -> p (t h)"), head_ms[:, :],
                                         half[:, 0:20], ALU.pow))
            step(nc.gpsimd.tensor_scalar(head_r[:, :, 0:HEADS_A], head_r[:, :, 0:HEADS_A],
                                         float(HD) ** -0.5, None, ALU.mult))
            n_heads = HEADS_A + KV_A
            step(nc.gpsimd.tensor_tensor(x, x, head_r[:, :, :].unsqueeze(3).to_broadcast([P, TOK, n_heads, HD]),
                                         ALU.mult))
            for g, (a, b) in enumerate(((0, HEADS_A), (HEADS_A, n_heads))):
                gain = gqk[:, HD * g:HD * g + HD].unsqueeze(1).unsqueeze(1).to_broadcast([P, TOK, b - a, HD])
                step(nc.gpsimd.tensor_tensor(x[:, :, a:b, :], x[:, :, a:b, :], gain, ALU.mult))
            pairs = projA[:, :, 0:QK_A].rearrange("p t (h c two) -> p t h c two", c=HD // 2, two=2)
            hc = [P, TOK, n_heads, HD // 2]
            half_n = TOK * n_heads * HD // 2
            prod = [tmpA[:, 0:half_n], tmpA[:, half_n:2 * half_n], stage[:, 0:half_n], work[:, 0:half_n]]
            prod = [a.rearrange("p (t h c) -> p t h c", t=TOK, h=n_heads) for a in prod]
            cos, sin = (ropeA[:, i].unsqueeze(2).to_broadcast(hc) for i in range(2))
            even, odd = pairs[:, :, :, :, 0], pairs[:, :, :, :, 1]
            step(nc.gpsimd.tensor_tensor(prod[0], even, cos, ALU.mult))
            step(nc.gpsimd.tensor_tensor(prod[1], odd, sin, ALU.mult))
            step(nc.gpsimd.tensor_tensor(prod[2], even, sin, ALU.mult))
            step(nc.gpsimd.tensor_tensor(prod[3], odd, cos, ALU.mult))
            step(nc.gpsimd.tensor_tensor(even, prod[0], prod[1], ALU.subtract))
            step(nc.gpsimd.tensor_tensor(odd, prod[2], prod[3], ALU.add))
            nc.gpsimd.memset(head_ms[:, 0:1], 0.0).then_inc(qk_ready, 1)
            pool.wait_ge(mix_evac, IN_A // 512 - 1)
            attention(HEADS_A, 0, False)
            inverse_rms(1)
            inverse_rms(2)

            pool.wait_ge(kr_out, 1)
            krp = kr.rearrange("p t (c two) -> p t c two", two=2)
            cos_c, sin_c = rope_c[:, 0, :, :], rope_c[:, 1, :, :]
            for i, (part, f) in enumerate(((0, cos_c), (1, sin_c), (0, sin_c), (1, cos_c))):
                step(nc.gpsimd.tensor_tensor(kr_tmp[:, i], krp[:, :, :, part], f, ALU.mult))
            step(nc.gpsimd.tensor_tensor(krp[:, :, :, 0], kr_tmp[:, 0], kr_tmp[:, 1], ALU.subtract))
            nc.gpsimd.tensor_tensor(krp[:, :, :, 1], kr_tmp[:, 2], kr_tmp[:, 3], ALU.add).then_inc(kr_roped, 1)

            pool.wait_ge(lat_sq, 4)
            r = rms[:, 2, :]
            for w in range(2):
                step(nc.gpsimd.tensor_tensor(lat_t[:, 0, w, :], lat_ss[:, w, :], r, ALU.mult))
                step(nc.gpsimd.tensor_tensor(lat_t[:, 1, w, :], lat_t[:, 0, w, :], r, ALU.mult))
                step(nc.gpsimd.tensor_scalar(lat_t[:, 2, w, :], lat_t[:, 1, w, :], 1.0 / LORA, NORM_EPS,
                                             ALU.mult, ALU.add))
                step(nc.gpsimd.tensor_tensor(lat_t[:, 0, w, :], lat_t[:, 2, w, :], half[:, 0:TOK], ALU.pow))
                if w == 0:
                    step(nc.gpsimd.tensor_scalar(lat_t[:, 0, w, :], lat_t[:, 0, w, :], float(QH) ** -0.5,
                                                 None, ALU.mult))
                ins = nc.gpsimd.tensor_tensor(lat_s[:, w, :], lat_t[:, 0, w, :], r, ALU.mult)
                if w == 0:
                    step(ins)
            ins.then_inc(lat_scale, 1)

            with nc.gpsimd.Fori(0, HEADS_C // 2 - 1) as it:
                rope_queries(0, it)
            pool.wait_ge(kv_out, HEADS_C // 2 - 1)
            attention(HEADS_C, HEADS_A, True)
            inverse_rms(3)

            pool.wait_ge(g_landed, 16)
            for t in range(TOK):
                for n in range(2):
                    c = slice(512 * n, 512 * n + 512)
                    pool.wait_ge(last_h, 4 * t + n + 1)
                    nc.gpsimd.tensor_tensor(final[:, t, c], h[:, t, c], g_final[:, c],
                                            ALU.mult).then_inc(gained, 1)
                pool.wait_ge(squares, TOK * 4 + t + 1)
                step(nc.gpsimd.tensor_scalar(meansq[:, 4, t:t + 1], sumsq[:, 4, t:t + 1], 1.0 / D, NORM_EPS,
                                             ALU.mult, ALU.add))
                nc.gpsimd.tensor_tensor(rms[:, 4, t:t + 1], meansq[:, 4, t:t + 1], half[:, 0:1],
                                        ALU.pow).then_inc(rms_ready, 1)


def turns(engine, n):
    for m in (-1, 0, 1):
        yield m, None
    with engine.Fori(0, (n - 4) // 2) as it:
        for m in (2, 3):
            yield m, it
    for m in range(n - 2, n + 2):
        yield m, None


_INS = ["x", "even_w_in", "even_q_norm_g", "even_k_norm_g", "even_w_out", "odd_w_down", "odd_w_uq",
        "odd_w_ukv", "odd_w_o", "mlp_w_up", "mlp_w_down", "final_norm_g"]

_GAINS = [("even_norm_g", 0), ("mlp_norm_g", 0), ("odd_norm_g", 0), ("mlp_norm_g", 1),
          ("odd_q_lat_g", 0), ("odd_kv_lat_g", 0), ("even_conv_w", 0)]


def _rope_table(np, rot_dim, grid_w=64):
    t = np.arange(T)
    axis = rot_dim // 2
    exponent = -np.arange(0, axis, 2, dtype=np.float32) / np.float32(axis)
    inv = np.power(np.float32(10000.0), exponent, dtype=np.float32)
    row, col = (t // grid_w).astype(np.float32), (t % grid_w).astype(np.float32)
    ang = np.concatenate([row[:, None] * inv, col[:, None] * inv], axis=-1)
    both = np.stack([np.cos(ang), np.sin(ang)]).astype(np.float32)
    return np.ascontiguousarray(both.reshape(2, TOK, P, -1).transpose(2, 0, 1, 3))


def kernel(**inputs):
    import numpy as _np
    import concourse.bacc as _bacc
    from concourse import mybir as _mybir
    from concourse.bass_utils import run_bass_kernel_spmd as _run

    nc = _bacc.Bacc("TRN2", target_bir_lowering=False, num_devices=1, dynamic_dma_scratch_size=1024)
    arrays, args = {}, {}

    def give(name, a):
        a = _np.ascontiguousarray(a)
        arrays[f"in_{name}_dram"] = a
        args[name] = nc.dram_tensor(f"in_{name}_dram", a.shape, _mybir.dt.from_np(a.dtype),
                                    kind="ExternalInput").ap()

    for name in _INS:
        give(name, inputs[name])
    give("gain_rows", _np.concatenate([_np.asarray(inputs[name])[i].reshape(-1, P) for name, i in _GAINS]))
    give("ident", _np.eye(P, dtype=_np.float32))
    give("rope_a", _rope_table(_np, HD))
    give("rope_c", _rope_table(_np, ROPE))
    out = nc.dram_tensor("out_0_dram", (1, T, D), F32, kind="ExternalOutput").ap()
    build(nc, args, out)
    r = _run(nc, [arrays], core_ids=[0])
    return r.results[0]["out_0_dram"]
```
